# Optimizing a Trainium2 kernel written in Bass

```python
import jax, jax.numpy as jnp
from jax import lax
import numpy as np

D_MODEL = 1024
BATCH = 1
SEQ = 2048
DEPTH = 1

CHUNK = 64
MIX_WIDTH = D_MODEL
RWKV_WIDTH = 512
RWKV_HEAD = 64
RWKV_HEADS = RWKV_WIDTH // RWKV_HEAD
DECAY_LORA = 64
AAA_LORA = 64
GATE_LORA = 128
SGU_WIDTH = MIX_WIDTH - RWKV_WIDTH
SGU_GROUPS = 8
SGU_BLOCK = 2 * CHUNK
RWKV_IN = 3 * RWKV_WIDTH + DECAY_LORA + AAA_LORA + GATE_LORA
IN_WIDTH = RWKV_IN + 2 * SGU_WIDTH
MEM_LEN = 256
XA_HEADS = 4
XA_HEAD_DIM = D_MODEL // XA_HEADS
D_FF = ((8 * D_MODEL // 3 + 255) // 256) * 256
RMS_EPS = 1e-6
LN_EPS = 1e-5
LNX_EPS = 64e-5

kernel_name = "hybrid_rwkv7_gmlp_memxattn_block"

def rmsnorm(x, g):
    xf = x.astype(jnp.float32)
    y = xf * lax.rsqrt(jnp.mean(xf * xf, axis=-1, keepdims=True) + RMS_EPS)
    return (y * g.astype(jnp.float32)).astype(x.dtype)

def token_shift(h):
    return jnp.pad(h, ((0, 0), (1, 0), (0, 0)))[:, :-1]

def wkv7_scan(r, w, k, v, kk, a):
    B, T, H, N = r.shape

    def step(S, inp):
        r_t, w_t, k_t, v_t, kk_t, a_t = inp
        sa = jnp.einsum('bhvk,bhk->bhv', S, -kk_t)
        S = (S * w_t[:, :, None, :]
             + sa[..., None] * (kk_t * a_t)[:, :, None, :]
             + v_t[..., None] * k_t[:, :, None, :])
        y = jnp.einsum('bhvk,bhk->bhv', S, r_t)
        return S, y

    xs = tuple(jnp.moveaxis(t, 1, 0) for t in (r, w, k, v, kk, a))
    S0 = jnp.zeros((B, H, N, N), jnp.float32)
    _, ys = lax.scan(step, S0, xs)
    return jnp.moveaxis(ys, 0, 1)

def rwkv7_group(h, shift_mu, w0, w_lora_up, a0, a_lora_up, g_lora_up, k_k, k_a, r_k, lnx_w, lnx_b):
    B, T, _ = h.shape
    f32 = jnp.float32
    h = h + (token_shift(h) - h) * shift_mu
    c = np.cumsum([RWKV_WIDTH, RWKV_WIDTH, RWKV_WIDTH, DECAY_LORA, AAA_LORA])
    r, k, v, wd, ad, gd = jnp.split(h, [int(i) for i in c], axis=-1)
    w_log = -jax.nn.softplus(-(w0 + jnp.tanh(wd) @ w_lora_up).astype(f32)) - 0.5
    decay = jnp.exp(-jnp.exp(w_log))
    a = jax.nn.sigmoid((a0 + ad @ a_lora_up).astype(f32))
    g = (jax.nn.sigmoid(gd) @ g_lora_up).astype(f32)
    heads = lambda t: t.reshape(B, T, RWKV_HEADS, RWKV_HEAD)
    kk = heads((k * k_k).astype(f32))
    kk = kk / jnp.maximum(jnp.sqrt(jnp.sum(kk * kk, axis=-1, keepdims=True)), 1e-12)
    k = k.astype(f32) * (1.0 + (a - 1.0) * k_a.astype(f32))
    rh, kh, vh = heads(r.astype(f32)), heads(k), heads(v.astype(f32))
    y = wkv7_scan(rh, heads(decay), kh, vh, kk, heads(a))
    mu = jnp.mean(y, axis=-1, keepdims=True)
    var = jnp.mean(jnp.square(y - mu), axis=-1, keepdims=True)
    y = ((y - mu) * lax.rsqrt(var + LNX_EPS)).reshape(B, T, RWKV_WIDTH)
    y = y * lnx_w.astype(f32) + lnx_b.astype(f32)
    bonus = (jnp.sum(rh * kh * r_k.astype(f32), axis=-1, keepdims=True) * vh).reshape(B, T, RWKV_WIDTH)
    return ((y + bonus) * g).astype(h.dtype)

def sgu_group(h, ln_w, ln_b, w_spatial, b_spatial):
    B, T, _ = h.shape
    u, v = jnp.split(jax.nn.gelu(h), 2, axis=-1)
    vf = v.astype(jnp.float32)
    mu = jnp.mean(vf, axis=-1, keepdims=True)
    var = jnp.mean(jnp.square(vf - mu), axis=-1, keepdims=True)
    v = ((vf - mu) * lax.rsqrt(var + LN_EPS) * ln_w + ln_b).astype(h.dtype)
    vb = v.reshape(B, T // SGU_BLOCK, SGU_BLOCK, SGU_GROUPS, SGU_WIDTH // SGU_GROUPS)
    mask = jnp.tril(jnp.ones((SGU_BLOCK, SGU_BLOCK), dtype=bool))
    ws = jnp.where(mask[None], w_spatial, jnp.zeros_like(w_spatial))
    mixed = jnp.einsum('gij,bnjgc->bnigc', ws, vb) + b_spatial.T[None, None, :, :, None]
    return u * mixed.reshape(B, T, SGU_WIDTH)

def mem_cross_attn(h, mem, mem_g, wq, wk, wv, wo):
    B, T, _ = h.shape
    m = rmsnorm(mem, mem_g)
    q = (h @ wq).reshape(B, T, XA_HEADS, XA_HEAD_DIM)
    k = (m @ wk).reshape(B, MEM_LEN, XA_HEADS, XA_HEAD_DIM)
    v = (m @ wv).reshape(B, MEM_LEN, XA_HEADS, XA_HEAD_DIM)
    s = jnp.einsum('bshd,bmhd->bhsm', q, k).astype(jnp.float32) * (XA_HEAD_DIM ** -0.5)
    p = jax.nn.softmax(s, axis=-1).astype(v.dtype)
    o = jnp.einsum('bhsm,bmhd->bshd', p, v).reshape(B, T, D_MODEL)
    return o @ wo

def swiglu(h, w_gate, w_up, w_down):
    return (jax.nn.silu(h @ w_gate) * (h @ w_up)) @ w_down

def setup_inputs(seed: int = 0) -> dict:
    key = jax.random.key(seed)
    ks = jax.random.split(key, 32)
    L = DEPTH
    nrm = lambda k, shape, s: jax.random.normal(k, shape, jnp.float32) * s
    gain = lambda k, shape: 1.0 + 0.02 * jax.random.normal(k, shape, jnp.float32)
    return {
        "x": nrm(ks[0], (BATCH, SEQ, D_MODEL), 1.0),
        "mem": nrm(ks[1], (BATCH, MEM_LEN, D_MODEL), 1.0),
        "norm1_g": gain(ks[2], (L, D_MODEL)),
        "w_in": nrm(ks[3], (L, D_MODEL, IN_WIDTH), D_MODEL ** -0.5),
        "shift_mu": jax.random.uniform(ks[4], (L, RWKV_IN), jnp.float32),
        "w0": jax.random.uniform(ks[5], (L, RWKV_WIDTH), jnp.float32, -5.0, 1.0),
        "w_lora_up": nrm(ks[6], (L, DECAY_LORA, RWKV_WIDTH), 0.1 * DECAY_LORA ** -0.5),
        "a0": nrm(ks[7], (L, RWKV_WIDTH), 0.1),
        "a_lora_up": nrm(ks[8], (L, AAA_LORA, RWKV_WIDTH), 0.1 * AAA_LORA ** -0.5),
        "g_lora_up": nrm(ks[9], (L, GATE_LORA, RWKV_WIDTH), GATE_LORA ** -0.5),
        "k_k": 0.85 + 0.05 * jax.random.normal(ks[10], (L, RWKV_WIDTH), jnp.float32),
        "k_a": 1.0 + 0.05 * jax.random.normal(ks[11], (L, RWKV_WIDTH), jnp.float32),
        "r_k": nrm(ks[12], (L, RWKV_HEADS, RWKV_HEAD), 0.1),
        "lnx_w": gain(ks[13], (L, RWKV_WIDTH)),
        "lnx_b": nrm(ks[14], (L, RWKV_WIDTH), 0.02),
        "sgu_ln_w": gain(ks[15], (L, SGU_WIDTH)),
        "sgu_ln_b": nrm(ks[16], (L, SGU_WIDTH), 0.02),
        "w_spatial": nrm(ks[17], (L, SGU_GROUPS, SGU_BLOCK, SGU_BLOCK), SGU_BLOCK ** -0.5),
        "b_spatial": gain(ks[18], (L, SGU_GROUPS, SGU_BLOCK)),
        "w_out": nrm(ks[19], (L, MIX_WIDTH, D_MODEL), MIX_WIDTH ** -0.5),
        "norm2_g": gain(ks[20], (L, D_MODEL)),
        "mem_norm_g": gain(ks[21], (L, D_MODEL)),
        "wq_x": nrm(ks[22], (L, D_MODEL, D_MODEL), D_MODEL ** -0.5),
        "wk_x": nrm(ks[23], (L, D_MODEL, D_MODEL), D_MODEL ** -0.5),
        "wv_x": nrm(ks[24], (L, D_MODEL, D_MODEL), D_MODEL ** -0.5),
        "wo_x": nrm(ks[25], (L, D_MODEL, D_MODEL), D_MODEL ** -0.5),
        "norm3_g": gain(ks[26], (L, D_MODEL)),
        "w_gate": nrm(ks[27], (L, D_MODEL, D_FF), D_MODEL ** -0.5),
        "w_up": nrm(ks[28], (L, D_MODEL, D_FF), D_MODEL ** -0.5),
        "w_down": nrm(ks[29], (L, D_FF, D_MODEL), D_FF ** -0.5),
        "norm_f_g": gain(ks[30], (D_MODEL,)),
    }

def reference(x, mem, norm1_g, w_in, shift_mu, w0, w_lora_up, a0, a_lora_up, g_lora_up,
              k_k, k_a, r_k, lnx_w, lnx_b, sgu_ln_w, sgu_ln_b, w_spatial, b_spatial, w_out,
              norm2_g, mem_norm_g, wq_x, wk_x, wv_x, wo_x, norm3_g, w_gate, w_up, w_down,
              norm_f_g):
    for l in range(DEPTH):
        z = rmsnorm(x, norm1_g[l]) @ w_in[l]
        y_rwkv = rwkv7_group(z[..., :RWKV_IN], shift_mu[l], w0[l], w_lora_up[l], a0[l],
                             a_lora_up[l], g_lora_up[l], k_k[l], k_a[l], r_k[l],
                             lnx_w[l], lnx_b[l])
        y_sgu = sgu_group(z[..., RWKV_IN:], sgu_ln_w[l], sgu_ln_b[l], w_spatial[l], b_spatial[l])
        x = x + jnp.concatenate([y_rwkv, y_sgu], axis=-1) @ w_out[l]
        x = x + mem_cross_attn(rmsnorm(x, norm2_g[l]), mem, mem_norm_g[l],
                               wq_x[l], wk_x[l], wv_x[l], wo_x[l])
        x = x + swiglu(rmsnorm(x, norm3_g[l]), w_gate[l], w_up[l], w_down[l])
    return rmsnorm(x, norm_f_g)


_drawn_inputs = setup_inputs


def setup_inputs(seed=0):
    import zlib

    import numpy as np

    out = dict(_drawn_inputs(seed))
    spreads = {}
    factors = {'norm1_g': 3.112,
     'w_lora_up': 8.0,
     'a0': 3.862,
     'a_lora_up': 4.026,
     'k_k': 4.011,
     'k_a': 3.089,
     'lnx_w': 8.0,
     'lnx_b': 8.0,
     'sgu_ln_w': 8.0,
     'sgu_ln_b': 8.0,
     'b_spatial': 6.979,
     'norm2_g': 8.0,
     'mem_norm_g': 8.0,
     'norm3_g': 13.656,
     'norm_f_g': 7.595}
    for name, (base, spread) in spreads.items():
        noise = np.random.default_rng([zlib.crc32(name.encode()), seed]).standard_normal(out[name].shape)
        drawn = base * np.exp(spread * noise) if base else spread * noise
        out[name] = __import__('jax').numpy.asarray(drawn.astype(out[name].dtype))
    for name, factor in factors.items():
        out[name] = (out[name] * factor).astype(out[name].dtype)
    return out
```

```python
import math
from contextlib import ExitStack

import concourse.bass as bass
from concourse import mybir

ALU = mybir.AluOpType
ACT = mybir.ActivationFunctionType
F32 = mybir.dt.float32
F32R = mybir.dt.float32r
U8 = mybir.dt.uint8
ds = bass.ds

P = 128
T = 2048
D = 1024
KT = D // P
TB = 1024
HALVES = T // TB
BANK = 512
NB = TB // BANK
MEM = 256
XH, XD = 4, 256
FF_TILES = 2816 // P
FF_GROUPS = (8, 8, 6)
assert sum(FF_GROUPS) == FF_TILES

RH, RN = 8, 64
L = 128
CHUNKS = T // L
HG = 4
LEVELS = (1, 2, 4, 8, 16, 32, 64)
DECAY = math.exp(-0.5)
SHIFT_TILES = 14
IN_TILES = 22
RMS_EPS, LN_EPS, LNX_EPS = 1e-6, 1e-5, 64e-5

PAIRS_MEM = 8
PAIRS_IN = IN_TILES // 2
PAIRS_OUT = 4
PAIRS_TAIL = 3 * PAIRS_OUT + FF_TILES + len(FF_GROUPS) * PAIRS_OUT
Q_IN = PAIRS_MEM
Q_TAIL = Q_IN + HALVES * PAIRS_IN
ROW_IN = 2 * PAIRS_MEM
ROW_TAIL = ROW_IN + IN_TILES

G_IN, G_ATT, G_FF, G_FINAL, G_MEM = range(5)


def hybrid_block_kernel(nc, xT, memT, gains, weights, shift_mu, w_lora, a_lora, g_lora, head_cols,
                        kk_rows, lnx_rows, kk_cols, rk_cols, w_spatialT, b_spatial, sgu_ln, consts, cen,
                        head_rows, head_mean, scan_reset, lower_masks, tri_masks, outT):
    with ExitStack() as ctx:
        base = (nc.sbuf_base + 63) // 64 * 64
        used = {}

        def place(name, shape, dt, off):
            size = 1
            for n in shape[1:]:
                size *= n
            size *= 1 if dt == U8 else 4
            used[name] = base + off + size
            return nc.alloc_sbuf_tensor_at(name, list(shape), dt, offset=base + off)

        sems = {}

        def sem(name):
            sems[name] = ctx.enter_context(nc.semaphore(name))
            return sems[name]

        KB = 1024
        OX, OA, OB, OW, OS = 0, 32 * KB, 96 * KB, 160 * KB, 184 * KB
        x = place("x", [P, KT, TB], F32, OX)
        a_hi = place("a_hi", [P, KT, TB], F32R, OA)
        a_lo = place("a_lo", [P, KT, TB], F32R, OA + 32 * KB)
        b_hi = place("b_hi", [P, KT, TB], F32R, OB)
        b_lo = place("b_lo", [P, KT, TB], F32R, OB + 32 * KB)
        w_raw = place("w_raw", [P, 2, KT, P], F32, OW)
        w_hi = place("w_hi", [P, 2, KT, P], F32R, OW + 8 * KB)
        w_lo = place("w_lo", [P, 2, KT, P], F32R, OW + 16 * KB)
        rstd = place("rstd", [P, TB], F32, OS)
        sumsq = place("sumsq", [P, TB], F32, OS + 4 * KB)
        sq = place("sq", [P, TB], F32, OS + 8 * KB)
        work = place("work", [P, 2, TB], F32, OS + 12 * KB)
        cst = place("cst", [P, 2, P], F32, OS + 20 * KB)
        gain = place("gain", [P, 5, KT], F32, OS + 21 * KB)
        mu = place("mu", [P, SHIFT_TILES], F32, OS + 21 * KB + 160)
        carry = place("carry", [P, SHIFT_TILES], F32, OS + 21 * KB + 224)
        stat_m = place("stat_m", [P, 2 * 4], F32, OS + 21 * KB + 288)
        stat_n = place("stat_n", [P, 2 * 4], F32, OS + 21 * KB + 320)
        stat_s = place("stat_s", [P, 2 * 4], F32, OS + 21 * KB + 352)
        stat_r = place("stat_r", [P, 2 * 4], F32, OS + 21 * KB + 384)
        eps = place("eps", [P, 4], F32, OS + 21 * KB + 416)
        ident, ones = cst[:, 0, :], cst[:, 1, :]
        in_raw = place("in_raw", [P, KT, TB], F32, OB)
        z_ext = place("z_ext", [P, 2, TB + 16], F32, OB + 32 * KB)
        z_out = place("z_out", [P, 2, TB], F32, OB + 32 * KB + 8320)
        mem_raw = place("mem_raw", [P, KT, MEM], F32, OB)
        vT = place("vT", [P, KT, MEM], F32, OB + 8 * KB)
        q = place("q", [P, KT, TB], F32, OA)
        kT = place("kT", [P, KT, MEM], F32, OA + 32 * KB)
        v = place("v", [P, 2, D], F32, OA + 40 * KB)
        prob = place("prob", [P, 2, 4, MEM], F32, OA + 48 * KB)
        probT = place("probT", [P, 2, 2, BANK], F32, OA + 56 * KB)
        kT0 = place("kT0", [P, KT, MEM], F32, OX)
        v0 = place("v0", [P, 2, D], F32, OX + 8 * KB)

        zT = nc.dram_tensor("zT", [IN_TILES * 2, RN, T], F32, kind="Internal").ap()
        yT = nc.dram_tensor("yT", [16, RN, T], F32, kind="Internal").ap()
        kT_d = nc.dram_tensor("kT_d", [P, KT * MEM], F32, kind="Internal").ap()
        v_d = nc.dram_tensor("v_d", [P, 2 * D], F32, kind="Internal").ap()
        zT_t = zT.rearrange("(m two) r t -> m (two r) t", two=2)
        yT_t = yT.rearrange("(k two) r t -> (two r) k t", two=2)

        ps = ctx.enter_context(nc.psum_tensor("ps", [P, 8, BANK], F32))

        roff = [0]

        def rw(name, shape, dt=F32):
            size = 1
            for n in shape[1:]:
                size *= n
            size = size * (1 if dt == U8 else 4)
            t = place(name, shape, dt, roff[0])
            roff[0] += (size + 31) // 32 * 32
            assert roff[0] <= OS + 20 * KB, (name, roff[0])
            return t

        low_in = place("low_in", [P, len(LEVELS) * 2 * HG * RN], F32, 0)
        tri_in = place("tri_in", [P, 2 * HG * L], F32, len(LEVELS) * 2 * HG * RN * 4)
        zin = [rw(f"zin{i}", [RN, 3, RH, L]) for i in range(2)]
        wd = [rw(f"wd{i}", [RN + 1, L]) for i in range(2)]
        ad = [rw(f"ad{i}", [RN + 1, L]) for i in range(2)]
        gd = [rw(f"gd{i}", [P, L]) for i in range(2)]
        su = [rw("su", [RN, RH, L])] * 2
        sv = [rw(f"sv{i}", [P, 4, L]) for i in range(2)]
        qr = [rw(f"qr{i}", [RN, RH, 2, L]) for i in range(2)]
        v_tok = [rw(f"v_tok{i}", [P, RH, RN]) for i in range(2)]
        k_tok = [rw(f"k_tok{i}", [P, RH, RN]) for i in range(2)]
        b_tok = [rw(f"b_tok{i}", [P, RH, RN]) for i in range(2)]
        gate = [rw("gate", [RN, RH, L])] * 2
        bonus = [rw(f"bonus{i}", [RN, RH, L]) for i in range(2)]
        w_mid = [rw(f"w_mid{i}", [RN, RH]) for i in range(2)]
        w_end = [rw(f"w_end{i}", [RN, RH]) for i in range(2)]
        sig_w = rw("sig_w", [RN, RH, L])
        a_t = rw("a_t", [RN, RH, L])
        cum = rw("cum", [RN, RH, L])
        cum_c = rw("cum_c", [RN, RH, L])
        w_neg = rw("w_neg", [RN, RH, L])
        k_sq = rw("k_sq", [RN, RH, L])
        kk = rw("kk", [RN, RH, L])
        k_mix = rw("k_mix", [RN, RH, L])
        rk = rw("rk", [RN, RH, L])
        n8 = rw("n8", [RH, 4, L])
        at = rw("at", [P, RH, L])
        rb = rw("rb", [P, RH, L])
        qk = rw("qk", [P, RH, L])
        rkm = rw("rkm", [P, RH, L])
        tm = rw("tm", [P, RH * L])
        um = rw("um", [P, RH * L])
        xm = rw("xm", [P, RH * L])
        rhs_t = rw("rhs_t", [P, RH, RN])
        sa_t = rw("sa_t", [P, RH, RN])
        h_st = rw("h_st", [RN, RH, RN])
        h_0 = rw("h_0", [RN, RH, RN])
        y_raw = rw("y_raw", [RN, RH, L])
        y_cen = rw("y_cen", [RN, RH, L])
        y_out = rw("y_out", [RN, RH, L])
        v_hat = rw("v_hat", [P, 4 * L])
        s_mix = rw("s_mix", [RN, RH, L])
        bn = rw("bn", [P, 12])
        wl = rw("wl", [RN + 1, RH * RN])
        al = rw("al", [RN + 1, RH * RN])
        gl = rw("gl", [P, RH * RN])
        hc = rw("hc", [RN, 3, RH])
        kkr = rw("kkr", [RH, RH, RN])
        lnr = rw("lnr", [RH, RH, RN])
        hr = rw("hr", [RH, RH, RN])
        kkc = rw("kkc", [RN, RH, RH])
        kkc2 = rw("kkc2", [RN, RH, RH])
        rkc = rw("rkc", [RN, RH, RH])
        hm = rw("hm", [RN, RH, RH])
        cent = rw("cent", [RN, RN])
        reset = rw("reset", [RN, RH * L])
        low = rw("low", [P, len(LEVELS), 2, HG * RN], U8)
        tri = rw("tri", [P, 2, HG * L], U8)
        ws = rw("ws", [P, RH, L])
        bsp = rw("bsp", [RN, RH, L])
        sln = rw("sln", [P, 2, 4 * L])
        cum_e, w_exc = sig_w, sig_w
        w_inc = cum_c
        k_new, b_vec = k_mix, a_t
        kt, bt = [k_mix] * 2, [a_t] * 2
        y_sq = k_sq
        y_n, y_b = y_cen, y_cen
        s_out = s_mix
        v_ln, v_lnb = v_hat, v_hat
        wsr = tm[:].rearrange("p (h t) -> p h t", t=L)
        for n, end in used.items():
            assert end <= nc.sbuf_usable_end, (n, end)

        for n in ("const_in w_raw0 w_raw1 w_hi_done w_lo_done job_done job_out act_in act_ready sq_done sumsq_done "
                  "stat_ps stat_rt rstd_done z_ext_done z_dif_done z_out_done z_st0 z_st1 carry_done zero_done "
                  "gelu_done kv_done v_tr v_trc kv_store kv_in q_done x_new sum_first act_hi act_lo gate_s gate_a up_s prod "
                  "prod_hi prod_lo s_ps s_max s_neg s_exp s_rcp s_nrm p_tr p_ev o_ps o_hi o_lo fin fin_st0 fin_st1 y_in half_end "
                  "rconst rconst_done masks_done su_in zin0 zin1 lora_in lw_ps la_ps lg_ps sw_done a_done gate_done ksq_done kn_ps kn_rt kn_mx kn_rc "
                  "kb_ps kk_done cum_done cumc_done cume_done w_done wend_done kmix_done knew_done kt_done bv_done bt_done qq_done "
                  "rr_done rk_done bon_ps bon_sb bonb_ps bon_v bonus_done vtr ktr btr vtc ktc btc "
                  "id_done sc_b sc_k sc_a ev_sc x_ps x_ev tu_ps tu_ev h0_done rhs_ps rhs_ev sa_ps sa_ev h_ps h_add h_new "
                  "y_ps y_ev yc_ps yc_cp yc_sq yv_ps yv_rt yv_rc yb_ps yn_done yb_done yo_done y_st "
                  "sg_tr sg_bn sg_ag sg_rt sg_rc sg_vh sg_lw sg_lb sg_ps sg_mx sg_out sg_st met_pe met_dve end_pool end_act end_pe end_dve").split():
            sem(n)
        S = sems

        def slot(j):
            return ps[:, 2 * j:2 * j + 2, :]

        def flat(ap):
            return ap.rearrange("p a b -> p (a b)")

        def left(t, b, h0, n):
            return t[:, h0 * L:(h0 + n) * L].rearrange("p (n two b) -> p n two b", two=2, b=b)[:, :, 0, :]

        def right(t, b, h0, n):
            return t[:, h0 * L:(h0 + n) * L].rearrange("p (n two b) -> p n two b", two=2, b=b)[:, :, 1, :]

        def heads(b0, rows=RN):
            return ps[0:rows, b0:b0 + 2, :].rearrange("p a (h t) -> p (a h) t", t=L)

        def met(eng):
            eng.sem_inc(S["met_pe" if eng.engine == mybir.EngineType.PE else "met_dve"], 1)

        block = ctx.enter_context(nc.Block())

        @block.sync
        def _(sp):
            def load_pair(pair, row, first=False):
                for u in range(2):
                    if not first:
                        sp.wait_ge(S["w_lo_done"], 2 * pair + u - 1)
                    sp.dma_start(w_raw[:, u:u + 1, :, :].rearrange("p a k m -> p a (k m)"),
                                 weights[ds(row + u, 1)].rearrange("a p n -> p a n")
                                 ).then_inc(S[f"w_raw{u}"], 16)

            for n in ("z_st0", "z_st1", "fin_st0", "fin_st1"):
                sp.sem_inc(S[n], 16)
            for dst, src in ((cst, consts), (gain, gains), (mu, shift_mu)):
                sp.dma_start(dst[:], src).then_inc(S["const_in"], 16)
            sp.dma_start(mem_raw[:], memT.rearrange("k p t -> p k t")).then_inc(S["act_in"], 16)
            load_pair(0, 0, first=True)
            with sp.Fori(1, PAIRS_MEM) as i:
                load_pair(i, 2 * i)
            sp.wait_ge(S["kv_done"], 8)
            sp.wait_ge(S["v_trc"], 4)
            sp.dma_start(kT_d, kT0[:].rearrange("p k t -> p (k t)")).then_inc(S["kv_store"], 16)
            sp.dma_start(v_d, v0[:].rearrange("p k t -> p (k t)")).then_inc(S["kv_store"], 16)
            sp.wait_ge(S["kv_store"], 32)

            with sp.Fori(0, HALVES) as hf:
                sp.wait_ge(S["half_end"], hf + 1)
                sp.dma_start(in_raw[:], xT[:, :, ds(hf * TB, TB)].rearrange("k p t -> p k t")
                             ).then_inc(S["act_in"], 16)
                load_pair(Q_IN + hf * PAIRS_IN, ROW_IN)

                def store_z(i, base_count):
                    for u in range(2):
                        if i is None:
                            continue
                        sp.wait_ge(S["z_out_done"], hf * IN_TILES + 2 * i + u + 1)
                        sp.dma_start(zT_t[ds(2 * i + u, 1), :, ds(hf * TB, TB)].rearrange("a p t -> p a t"),
                                     z_out[:, u:u + 1, :]).then_inc(S[f"z_st{u}"], 16)

                with sp.Fori(1, PAIRS_IN) as i:
                    load_pair(Q_IN + hf * PAIRS_IN + i, ROW_IN + 2 * i)
                    store_z(i - 1, 0)
                for u in range(2):
                    sp.wait_ge(S["z_out_done"], hf * IN_TILES + IN_TILES - 1 + u)
                    sp.dma_start(zT_t[IN_TILES - 2 + u:IN_TILES - 1 + u, :, ds(hf * TB, TB)].rearrange("a p t -> p a t"),
                                 z_out[:, u:u + 1, :]).then_inc(S[f"z_st{u}"], 16)
            for u in range(2):
                sp.wait_ge(S[f"z_st{u}"], 16 * (1 + HALVES * PAIRS_IN))

            sp.wait_ge(S["job_out"], 2 * Q_TAIL)
            for dst, src in ((wl, w_lora), (al, a_lora), (gl, g_lora), (hc, head_cols), (kkr, kk_rows), (lnr, lnx_rows),
                             (hr, head_rows), (kkc, kk_cols), (rkc, rk_cols), (hm, head_mean), (cent, cen),
                             (reset, scan_reset), (low_in, lower_masks), (tri_in, tri_masks)):
                sp.dma_start(dst[:], src).then_inc(S["rconst"], 16)
            sp.dma_start(wsr, w_spatialT).then_inc(S["rconst"], 16)
            sp.dma_start(bsp[:], b_spatial.partition_broadcast(RN)).then_inc(S["rconst"], 16)
            sp.dma_start(sln[:], sgu_ln.partition_broadcast(P)).then_inc(S["rconst"], 16)

            def load_chunk(c, par, first):
                if not first:
                    for e in ("pool", "act", "pe", "dve"):
                        sp.wait_ge(S["end_" + e], c - 1)
                n = S[f"zin{par}"]
                at_c = ds(c * L, L)
                for s in range(3):
                    sp.dma_start(zin[par][:, s, :, :], zT[s * RH:(s + 1) * RH, :, at_c].rearrange("h r t -> r h t")).then_inc(n, 16)
                sp.dma_start(wd[par][0:RN, :], zT[24, :, at_c]).then_inc(n, 16)
                sp.dma_start(ad[par][0:RN, :], zT[25, :, at_c]).then_inc(n, 16)
                sp.dma_start(gd[par][:], zT_t[13, :, at_c]).then_inc(n, 16)
                sp.dma_start(sv[par][:], zT_t[18:22, :, at_c].rearrange("m p t -> p m t")).then_inc(n, 16)

            def load_u(c, first=False):
                if not first:
                    sp.wait_ge(S["sg_out"], c)
                sp.dma_start(su[0][:], zT[28:36, :, ds(c * L, L)].rearrange("h r t -> r h t")).then_inc(S["su_in"], 16)

            def store_chunk(c):
                sp.wait_ge(S["yo_done"], c + 1)
                sp.dma_start(yT[0:8, :, ds(c * L, L)].rearrange("h r t -> r h t"), y_out[:]).then_inc(S["y_st"], 16)
                sp.wait_ge(S["sg_out"], c + 1)
                sp.dma_start(yT[8:16, :, ds(c * L, L)].rearrange("h r t -> r h t"), s_out[:]).then_inc(S["sg_st"], 16)

            sp.wait_ge(S["masks_done"], 2)
            load_chunk(0, 0, True)
            load_u(0, True)
            load_chunk(1, 1, True)
            store_chunk(0)
            load_u(1)
            store_chunk(1)
            with sp.Fori(1, CHUNKS // 2) as i:
                for par in range(2):
                    load_chunk(2 * i + par, par, False)
                for par in range(2):
                    load_u(2 * i + par)
                    store_chunk(2 * i + par)
            sp.wait_ge(S["y_st"], 16 * CHUNKS)
            sp.wait_ge(S["sg_st"], 16 * CHUNKS)
            for e in ("pool", "act", "pe", "dve"):
                sp.wait_ge(S["end_" + e], CHUNKS)

            sp.dma_start(cst[:], consts).then_inc(S["const_in"], 16)
            with sp.Fori(0, HALVES) as hf:
                base_q = Q_TAIL + hf * PAIRS_TAIL
                sp.wait_ge(S["half_end"], HALVES + 2 + hf)
                sp.dma_start(in_raw[:], yT_t[:, :, ds(hf * TB, TB)]).then_inc(S["y_in"], 16)
                sp.dma_start(x[:], xT[:, :, ds(hf * TB, TB)].rearrange("k p t -> p k t")).then_inc(S["y_in"], 16)
                with sp.Fori(0, 2 * PAIRS_OUT) as i:
                    load_pair(base_q + i, ROW_TAIL + 2 * i)
                sp.wait_ge(S["job_done"], 2 * (base_q + PAIRS_OUT))
                sp.dma_start(kT[:].rearrange("p k t -> p (k t)"), kT_d).then_inc(S["kv_in"], 16)
                sp.dma_start(v[:].rearrange("p k t -> p (k t)"), v_d).then_inc(S["kv_in"], 16)
                with sp.Fori(2 * PAIRS_OUT, PAIRS_TAIL) as i:
                    load_pair(base_q + i, ROW_TAIL + 2 * i)

                with sp.Fori(0, KT // 2) as i:
                    for u in range(2):
                        sp.wait_ge(S["fin"], hf * KT + 2 * i + u + 1)
                        sp.dma_start(outT[ds(2 * i + u, 1), :, ds(hf * TB, TB)].rearrange("k p t -> p k t"),
                                     work[:, u:u + 1, :]).then_inc(S[f"fin_st{u}"], 16)
            for u in range(2):
                sp.wait_ge(S[f"fin_st{u}"], 16 * (1 + HALVES * KT // 2))

        @block.gpsimd
        def _(pool):
            def split_pair(pair):
                for u in range(2):
                    split_job(pair, u)

            def split_job(pair, u):
                pool.wait_ge(S["w_hi_done"], 2 * pair + u + 1)
                pool.tensor_tensor(w_lo[:, u, :, :], w_raw[:, u, :, :], w_hi[:, u, :, :].bitcast(F32),
                                   ALU.subtract).then_inc(S["w_lo_done"], 1)

            def square_tile(src, count, first, k_expr):
                if first:
                    pool.tensor_tensor(sumsq[:, 0:src.shape[-1]], src, src, ALU.mult).then_inc(S["sumsq_done"], 1)
                else:
                    pool.wait_ge(S["sumsq_done"], count[1])
                    pool.tensor_tensor(sq[:, 0:src.shape[-1]], src, src, ALU.mult).then_inc(S["sq_done"], 1)
                    pool.wait_ge(S["sq_done"], count[0])
                    pool.tensor_tensor(sumsq[:, 0:src.shape[-1]], sumsq[:, 0:src.shape[-1]], sq[:, 0:src.shape[-1]],
                                       ALU.add).then_inc(S["sumsq_done"], 1)

            pool.memset(carry[:], 0.0).then_inc(S["zero_done"], 1)
            pool.memset(eps[:, 0:1], RMS_EPS).then_inc(S["zero_done"], 1)
            pool.memset(eps[:, 1:2], LN_EPS).then_inc(S["zero_done"], 1)
            pool.memset(eps[:, 2:3], LNX_EPS).then_inc(S["zero_done"], 1)
            pool.wait_ge(S["act_in"], 16)
            square_tile(mem_raw[:, 0, :], None, True, 0)
            for k in range(1, KT):
                square_tile(mem_raw[:, k, :], (k, k), False, k)
            with pool.Fori(0, PAIRS_MEM) as i:
                split_pair(i)
            with pool.Fori(0, HALVES) as hf:
                pool.wait_ge(S["act_in"], 32 + 16 * hf)
                pool.wait_ge(S["stat_ps"], 1 + hf)
                square_tile(in_raw[:, 0, :], None, True, 0)
                for k in range(1, KT):
                    square_tile(in_raw[:, k, :], ((1 + hf) * (KT - 1) + k, (1 + hf) * KT + k), False, k)
                with pool.Fori(0, PAIRS_IN) as i:
                    split_pair(Q_IN + hf * PAIRS_IN + i)

            pool.wait_ge(S["rconst"], 16 * 17)
            pool.memset(ws[:], 0.0).then_inc(S["rconst_done"], 1)
            for t in (at, rb, qk, rkm):
                pool.memset(t[:], 0.0).then_inc(S["rconst_done"], 1)
            pool.memset(xm[:], 0.0).then_inc(S["rconst_done"], 1)
            pool.memset(h_st[:], 0.0).then_inc(S["rconst_done"], 1)
            pool.wait_ge(S["rconst_done"], 7)
            for par in range(2):
                pool.wait_ge(S["rconst_done"], 7 + 2 * par)
                pool.memset(wd[par][RN:RN + 1, :], 1.0).then_inc(S["rconst_done"], 1)
                pool.wait_ge(S["rconst_done"], 8 + 2 * par)
                pool.memset(ad[par][RN:RN + 1, :], 1.0).then_inc(S["rconst_done"], 1)

            def mixer(c, par, first):
                r_in, k_in = zin[par][:, 0, :, :], zin[par][:, 1, :, :]
                pool.wait_ge(S["cumc_done"], c + 1)
                pool.wait_ge(S["sw_done"], 2 * c + 2)
                pool.wait_ge(S["cum_done"], c + 1)
                pool.tensor_tensor(cum_e[:], cum_c[:], sig_w[:], ALU.subtract).then_inc(S["cume_done"], 1)
                pool.wait_ge(S["kmix_done"], 8 * c + 8)
                pool.tensor_tensor(k_new[:], k_in, k_mix[:], ALU.mult).then_inc(S["knew_done"], 1)
                pool.wait_ge(S["knew_done"], c + 1)
                if not first:
                    pool.wait_ge(S["bon_ps"], c)
                pool.tensor_tensor(rk[:], r_in, k_new[:], ALU.mult).then_inc(S["rk_done"], 1)
                pool.wait_ge(S["kk_done"], 2 * c + 2)
                pool.wait_ge(S["a_done"], 2 * c + 2)
                pool.wait_ge(S["kmix_done"], 8 * c + 8)
                pool.tensor_tensor(b_vec[:], kk[:], a_t[:], ALU.mult).then_inc(S["bv_done"], 1)
                pool.wait_ge(S["w_done"], 4 * c + 3)
                pool.wait_ge(S["rk_done"], c + 1)
                pool.tensor_tensor(kt[par][:], k_new[:], w_neg[:], ALU.mult).then_inc(S["kt_done"], 1)
                pool.tensor_tensor(qr[par][:, :, 1, :], r_in, w_inc[:], ALU.mult).then_inc(S["rr_done"], 1)
                pool.wait_ge(S["bon_v"], 2 * c + 2)
                pool.tensor_tensor(bonus[par][:], bonus[par][:], hc[:, 2, :].unsqueeze(2).to_broadcast([RN, RH, L]),
                                   ALU.add).then_inc(S["bonus_done"], 1)
                pool.wait_ge(S["sg_vh"], c + 1)
                pool.tensor_tensor(v_ln[:], v_hat[:], sln[:, 0, :], ALU.mult).then_inc(S["sg_lw"], 1)
                pool.wait_ge(S["sg_lw"], c + 1)
                pool.tensor_tensor(v_lnb[:], v_ln[:], sln[:, 1, :], ALU.add).then_inc(S["sg_lb"], 1)
                pool.wait_ge(S["sg_mx"], 2 * c + 2)
                pool.wait_ge(S["su_in"], 16 * (c + 1))
                pool.tensor_tensor(s_out[:], s_mix[:], su[par][:], ALU.mult).then_inc(S["sg_out"], 1)
                pool.wait_ge(S["yn_done"], 2 * c + 2)
                pool.wait_ge(S["bonus_done"], c + 1)
                pool.tensor_tensor(y_b[:], y_n[:], bonus[par][:], ALU.add).then_inc(S["yb_done"], 1)
                pool.wait_ge(S["yb_done"], c + 1)
                pool.wait_ge(S["gate_done"], 2 * c + 2)
                if not first:
                    pool.wait_ge(S["y_st"], 16 * c)
                pool.tensor_tensor(y_out[:], y_b[:], gate[par][:], ALU.mult).then_inc(S["yo_done"], 1)
                pool.wait_ge(S["yo_done"], c + 1)
                pool.sem_inc(S["end_pool"], 1)

            mixer(0, 0, True)
            mixer(1, 1, False)
            with pool.Fori(1, CHUNKS // 2) as i:
                for par in range(2):
                    mixer(2 * i + par, par, False)

            norms = 1 + HALVES
            with pool.Fori(0, HALVES) as hf:
                base_q = Q_TAIL + hf * PAIRS_TAIL
                base_x = hf * 3 * KT
                done = norms + 3 * hf

                def squares(n, i, u, k, first=False):
                    pool.wait_ge(S["x_new"], base_x + n * KT + k + 1)
                    if first:
                        pool.wait_ge(S["stat_ps"], done + n)
                    square_tile(x[:, ds(k, 1), :] if not isinstance(k, int) else x[:, k:k + 1, :],
                                ((done + n) * (KT - 1) + k, (done + n) * KT + k), first, k)

                def squares_phase(n, q0, q_next):
                    split_pair(q0 + 1)
                    squares(n, 0, 0, 0, True)
                    squares(n, 0, 1, 1)
                    with pool.Fori(2, PAIRS_OUT) as i:
                        split_pair(q0 + i)
                        squares(n, 0, 0, 2 * i - 2)
                        squares(n, 0, 1, 2 * i - 1)
                    if q_next is not None:
                        split_pair(q_next)
                    squares(n, 0, 0, KT - 2)
                    squares(n, 0, 1, KT - 1)

                split_pair(base_q)
                squares_phase(0, base_q, base_q + PAIRS_OUT)
                with pool.Fori(PAIRS_OUT + 1, 2 * PAIRS_OUT + 1) as i:
                    split_pair(base_q + i)
                squares_phase(1, base_q + 2 * PAIRS_OUT, base_q + 3 * PAIRS_OUT)
                with pool.Fori(3 * PAIRS_OUT + 1, PAIRS_TAIL - PAIRS_OUT + 1) as i:
                    split_pair(base_q + i)
                squares_phase(2, base_q + PAIRS_TAIL - PAIRS_OUT, None)

        @block.scalar
        def _(act):
            def hi(pair, u, first=False):
                act.wait_ge(S[f"w_raw{u}"], 16 * (pair + 1))
                if not first:
                    act.wait_ge(S["job_done"], 2 * pair + u - 1)
                act.activation(w_hi[:, u, :, :], w_raw[:, u, :, :], ACT.Copy).then_inc(S["w_hi_done"], 1)

            def split_rms(n, stat_cols=TB):
                act.wait_ge(S["stat_ps"], n + 1)
                act.activation(sq_rt(stat_cols), stat_psum(stat_cols), ACT.Sqrt, bias=eps[:, 0:1], scale=1.0 / D
                               ).then_inc(S["stat_rt"], 1)

            def sq_rt(cols):
                return rstd[:, 0:cols]

            def stat_psum(cols):
                return ps[:, 4:6, :].rearrange("p a b -> p (a b)")[:, 0:cols]

            act.wait_ge(S["zero_done"], 4)
            act.wait_ge(S["const_in"], 48)
            act.wait_ge(S["act_in"], 16)
            for k in range(KT):
                act.activation(a_hi[:, k, 0:MEM], mem_raw[:, k, :], ACT.Copy, scale=gain[:, G_MEM, k:k + 1]
                               ).then_inc(S["act_hi"], 1)
            hi(0, 0, True)
            hi(0, 1, True)
            split_rms(0, MEM)
            with act.Fori(1, PAIRS_MEM) as i:
                hi(i, 0)
                hi(i, 1)

            with act.Fori(0, HALVES) as hf:
                act.wait_ge(S["act_in"], 32 + 16 * hf)
                act.wait_ge(S["job_done"], 2 * (Q_IN + hf * PAIRS_IN))
                for k in range(KT):
                    act.activation(a_hi[:, k, :], in_raw[:, k, :], ACT.Copy, scale=gain[:, G_IN, k:k + 1]
                                   ).then_inc(S["act_hi"], 1)
                q0 = Q_IN + hf * PAIRS_IN
                hi(q0, 0)
                hi(q0, 1)
                act.wait_ge(S["job_out"], 2 * q0)
                split_rms(1 + hf)
                with act.Fori(1, SHIFT_TILES // 2 + 1) as i:
                    hi(q0 + i, 0)
                    hi(q0 + i, 1)

                def gelu(i, u):
                    m = 2 * i + u
                    act.wait_ge(S["z_ext_done"], hf * IN_TILES + m + 1)
                    act.wait_ge(S[f"z_st{u}"], 16 * (1 + hf * PAIRS_IN + i))
                    act.activation(z_out[:, u, :], z_ext[:, u, 1:TB + 1], ACT.Gelu_apprx_tanh).then_inc(S["z_out_done"], 1)

                with act.Fori(SHIFT_TILES // 2 + 1, PAIRS_IN) as i:
                    for u in range(2):
                        hi(q0 + i, u)
                        gelu(i - 1, u)
                for u in range(2):
                    gelu(PAIRS_IN - 1, u)

            def mixer(c, par, first):
                k_in = zin[par][:, 1, :, :]
                half_c = i_of[0]
                act.wait_ge(S[f"zin{par}"], 16 * 7 * (1 if isinstance(c, int) else half_c + 1))
                act.activation(wd[par][0:RN, :], wd[par][0:RN, :], ACT.Tanh).then_inc(S["lora_in"], 1)
                act.activation(gd[par][:], gd[par][:], ACT.Sigmoid).then_inc(S["lora_in"], 1)
                if not first:
                    act.wait_ge(S["yv_ps"], c)
                act.activation(k_sq[:], k_in, ACT.Square).then_inc(S["ksq_done"], 1)
                for dst, src_ps, done in ((sig_w, "lw_ps", "sw_done"), (a_t, "la_ps", "a_done")):
                    if not first:
                        act.wait_ge(S["btr"], c)
                        act.wait_ge(S["sc_a"], 2 * c)
                        act.wait_ge(S["bv_done"], c)
                        act.wait_ge(S["cume_done"], c)
                        act.wait_ge(S["bt_done"], c)
                        act.wait_ge(S["qq_done"], c)
                    for hh in range(2):
                        act.wait_ge(S[src_ps], 2 * c + hh + 1)
                        act.activation(dst[:, HG * hh:HG * hh + HG, :], ps[0:RN, 6 + hh, :].rearrange("p (h t) -> p h t", t=L),
                                       ACT.Sigmoid).then_inc(S[done], 1)
                if not first:
                    act.wait_ge(S["yo_done"], c)
                for hh in range(2):
                    act.wait_ge(S["lg_ps"], 2 * c + hh + 1)
                    act.activation(gate[par][:, HG * hh:HG * hh + HG, :], ps[0:RN, 6 + hh, :].rearrange("p (h t) -> p h t", t=L),
                                   ACT.Copy).then_inc(S["gate_done"], 1)
                act.wait_ge(S["kn_ps"], c + 1)
                act.activation(n8[:, 0, :], ps[0:RH, 6, 0:L], ACT.Sqrt).then_inc(S["kn_rt"], 1)
                act.wait_ge(S["sg_ag"], c + 1)
                act.activation(bn[:, 8:9], bn[:, 7:8], ACT.Sqrt, bias=eps[:, 1:2]).then_inc(S["sg_rt"], 1)
                act.wait_ge(S["cumc_done"], c + 1)
                if not first:
                    act.wait_ge(S["bt_done"], c)
                    act.wait_ge(S["kt_done"], c)
                act.activation(w_neg[:], cum_c[:], ACT.Exp, scale=DECAY).then_inc(S["w_done"], 1)
                act.wait_ge(S["cume_done"], c + 1)
                act.activation(w_inc[:], cum_c[:], ACT.Exp, scale=-DECAY).then_inc(S["w_done"], 1)
                act.activation(w_mid[par][:], cum[:, :, RN - 1], ACT.Exp, scale=-DECAY).then_inc(S["w_done"], 1)
                act.wait_ge(S["cume_done"], c + 1)
                act.activation(w_exc[:], cum_e[:], ACT.Exp, scale=-DECAY).then_inc(S["w_done"], 1)
                act.wait_ge(S["w_done"], 4 * c + 4)
                act.activation(w_end[par][:], w_inc[:, :, L - 1], ACT.Copy).then_inc(S["wend_done"], 1)
                act.wait_ge(S["bon_ps"], c + 1)
                act.activation(n8[:, 3, :], ps[0:RH, 6, 0:L], ACT.Copy).then_inc(S["bon_sb"], 1)
                for dst, tr, done, bank in ((v_tok, "vtr", "vtc", 7), (k_tok, "ktr", "ktc", 6), (b_tok, "btr", "btc", 7)):
                    act.wait_ge(S[tr], c + 1)
                    act.activation(dst[par][:].rearrange("p h r -> p (h r)"), ps[:, bank, :], ACT.Copy).then_inc(S[done], 1)
                if not first:
                    act.wait_ge(S["sa_ps"], c)
                    act.wait_ge(S["tu_ps"], 12 * c)
                for g in range(2):
                    act.activation(tm[:, g * HG * L:(g + 1) * HG * L].rearrange("p (h t) -> p h t", t=L),
                                   ident.unsqueeze(1).to_broadcast([P, HG, L]), ACT.Copy).then_inc(S["id_done"], 1)
                    act.activation(um[:, g * HG * L:(g + 1) * HG * L].rearrange("p (h t) -> p h t", t=L),
                                   ident.unsqueeze(1).to_broadcast([P, HG, L]), ACT.Copy).then_inc(S["id_done"], 1)
                for lv in range(1, len(LEVELS)):
                    for g in range(2):
                        act.wait_ge(S["x_ps"], 12 * c + 2 * lv - 2 + g + 1)
                        act.activation(left(xm, LEVELS[lv], g * HG, HG),
                                       ps[:, g, 0:HG * RN].rearrange("p (n b) -> p n b", b=LEVELS[lv]),
                                       ACT.Copy).then_inc(S["x_ev"], 1)
                act.wait_ge(S["sa_ps"], c + 1)
                if not first:
                    act.wait_ge(S["y_ps"], 2 * c)
                act.activation(sa_t[:].rearrange("p h r -> p (h r)"), ps[:, 5, :], ACT.Copy).then_inc(S["sa_ev"], 1)
                for hh in range(2):
                    act.wait_ge(S["y_ps"], 2 * c + hh + 1)
                    act.activation(y_raw[:, HG * hh:HG * hh + HG, :], ps[0:RN, hh, :].rearrange("p (h t) -> p h t", t=L),
                                   ACT.Copy).then_inc(S["y_ev"], 1)
                for hh in range(2):
                    act.wait_ge(S["yc_ps"], 2 * c + hh + 1)
                    if not first:
                        act.wait_ge(S["yo_done"], c)
                    act.activation(y_cen[:, HG * hh:HG * hh + HG, :], ps[0:RN, 2 + hh, :].rearrange("p (h t) -> p h t", t=L),
                                   ACT.Copy).then_inc(S["yc_cp"], 1)
                    act.activation(y_sq[:, HG * hh:HG * hh + HG, :], ps[0:RN, 2 + hh, :].rearrange("p (h t) -> p h t", t=L),
                                   ACT.Square).then_inc(S["yc_sq"], 1)
                act.wait_ge(S["yv_ps"], c + 1)
                act.activation(n8[:, 2, :], ps[0:RH, 4, 0:L], ACT.Sqrt, bias=eps[0:RH, 2:3]).then_inc(S["yv_rt"], 1)
                act.wait_ge(S["yv_rt"], c + 1)
                act.sem_inc(S["end_act"], 1)

            act.wait_ge(S["rconst_done"], 11 + 3)
            i_of = [0]
            mixer(0, 0, True)
            mixer(1, 1, False)
            with act.Fori(1, CHUNKS // 2) as i:
                i_of[0] = i
                for par in range(2):
                    mixer(2 * i + par, par, False)

            act.wait_ge(S["const_in"], 64)
            act_parts = 8 * (1 + HALVES)
            with act.Fori(0, HALVES) as hf:
                q0 = Q_TAIL + hf * PAIRS_TAIL
                n0 = 1 + HALVES + 3 * hf
                base_hi = act_parts + hf * 3 * KT
                base_x = hf * 3 * KT
                act.wait_ge(S["y_in"], 32 * (hf + 1))
                act.wait_ge(S["job_done"], 2 * q0)
                for k in range(KT):
                    act.activation(a_hi[:, k, :], in_raw[:, k, :], ACT.Copy).then_inc(S["act_hi"], 1)
                hi(q0, 0)
                hi(q0, 1)

                def split_x(n, k, dst, g):
                    act.wait_ge(S["x_new"], base_x + n * KT + k + 1)
                    act.activation(dst[:, ds(k, 1), :] if not isinstance(k, int) else dst[:, k:k + 1, :],
                                   x[:, ds(k, 1), :] if not isinstance(k, int) else x[:, k:k + 1, :], ACT.Copy,
                                   scale=gain[:, g, ds(k, 1)] if not isinstance(k, int) else gain[:, g, k:k + 1]
                                   ).then_inc(S["act_hi"], 1)

                def residual_phase(n, first_q, dst, g):
                    with act.Fori(1, PAIRS_OUT) as i:
                        for u in range(2):
                            hi(first_q + i, u)
                            split_x(n, 2 * i - 2 + u, dst, g)
                    for u in range(2):
                        hi(first_q + PAIRS_OUT, u)
                        split_x(n, KT - 2 + u, dst, g)

                residual_phase(0, q0, b_hi, G_ATT)
                act.wait_ge(S["half_end"], HALVES + 2 + hf)
                split_rms(n0)
                with act.Fori(1, PAIRS_OUT) as i:
                    for u in range(2):
                        hi(q0 + PAIRS_OUT + i, u)
                for u in range(2):
                    hi(q0 + 2 * PAIRS_OUT, u)
                def exps(unit):
                    for t in range(4):
                        c = 4 * (unit % 2) + t
                        act.wait_ge(S["s_neg"], hf * 8 + unit + 1)
                        if unit >= 2:
                            act.wait_ge(S["p_tr"], hf * 8 + unit - 1)
                            act.wait_ge(S["s_rcp"], hf * 8 + unit - 1)
                        act.activation(prob[:, unit % 2, t, :],
                                       ps[:, 2 * (unit % 2) + t // 2, (t % 2) * MEM:(t % 2 + 1) * MEM], ACT.Exp,
                                       bias=stat_n[:, c:c + 1], scale=float(XD) ** -0.5, accum_out=stat_s[:, c:c + 1]
                                       ).then_inc(S["s_exp"], 1)

                def probs_out(unit):
                    act.wait_ge(S["p_tr"], hf * 8 + unit + 1)
                    if unit >= 2:
                        act.wait_ge(S["o_ps"], hf * 8 + unit - 1)
                    act.activation(probT[:, unit % 2, :, :], ps[:, 4:6, :], ACT.Copy).then_inc(S["p_ev"], 1)

                def out_hi(unit):
                    h, nb = unit // NB, unit % NB
                    act.wait_ge(S["o_ps"], hf * 8 + unit + 1)
                    act.activation(b_hi[:, 2 * h:2 * h + 2, nb * BANK:(nb + 1) * BANK], ps[:, 6:8, :], ACT.Copy
                                   ).then_inc(S["o_hi"], 1)

                for unit in range(8):
                    exps(unit)
                    probs_out(unit)
                    if unit:
                        out_hi(unit - 1)
                out_hi(7)
                residual_phase(1, q0 + 2 * PAIRS_OUT, a_hi, G_FF)
                split_rms(n0 + 1)
                def product(f_all, f):
                    act.wait_ge(S["gate_s"], hf * FF_TILES + f_all + 1)
                    act.activation(work[:, 0, :], work[:, 0, :], ACT.Silu).then_inc(S["gate_a"], 1)
                    act.wait_ge(S["prod"], hf * FF_TILES + f_all + 1)
                    act.activation(b_hi[:, ds(f, 1), :] if not isinstance(f, int) else b_hi[:, f:f + 1, :],
                                   work[:, 1:2, :], ACT.Copy).then_inc(S["prod_hi"], 1)

                at_q, f0 = 3 * PAIRS_OUT, 0
                for gi, n in enumerate(FF_GROUPS):
                    with act.Fori(1, n) as i:
                        hi(q0 + at_q + i, 0)
                        hi(q0 + at_q + i, 1)
                        product(f0 + i - 1, i - 1)
                    last = gi == len(FF_GROUPS) - 1
                    hi(q0 + at_q + n, 0)
                    hi(q0 + at_q + n, 1)
                    product(f0 + n - 1, n - 1)
                    with act.Fori(1, PAIRS_OUT + (not last)) as i:
                        hi(q0 + at_q + n + i, 0)
                        hi(q0 + at_q + n + i, 1)
                    at_q += n + PAIRS_OUT
                    f0 += n
                act.wait_ge(S["job_out"], 2 * (q0 + PAIRS_TAIL))
                split_rms(n0 + 2)

        @block.tensor
        def _(pe):
            def job(pair, u, hi_in, lo_in, kn, cols=TB, first=False):
                pe.wait_ge(S["w_lo_done"], 2 * pair + u + 1)
                if not first:
                    pe.wait_ge(S["job_out"], 2 * pair + u - 1)
                nbs = max(1, cols // BANK)
                w = min(cols, BANK)
                for k in range(kn):
                    for wt, rs in ((w_hi, (hi_in, lo_in)), (w_lo, (hi_in,))):
                        for nb in range(nbs):
                            for r in rs:
                                mm = pe.matmul(slot(u)[:, nb, 0:w], wt[:, u, k, :], r[:, k, nb * w:(nb + 1) * w],
                                               start=(k == 0 and r is hi_in and wt is w_hi),
                                               stop=(k == kn - 1 and wt is w_lo))
                mm.then_inc(S["job_done"], 1)

            def stats(n, cols=TB):
                pe.wait_ge(S["sumsq_done"], KT * (n + 1))
                for nb in range(max(1, cols // BANK)):
                    w = min(cols, BANK)
                    mm = pe.matmul(ps[:, 4 + nb, 0:w], ones, sumsq[:, nb * w:(nb + 1) * w], start=True, stop=True)
                mm.then_inc(S["stat_ps"], 1)

            pe.wait_ge(S["const_in"], 48)
            stats(0, MEM)
            pe.wait_ge(S["act_lo"], KT)
            job(0, 0, a_hi, a_lo, KT, MEM, True)
            job(0, 1, a_hi, a_lo, KT, MEM, True)
            with pe.Fori(1, PAIRS_MEM) as i:
                job(i, 0, a_hi, a_lo, KT, MEM)
                job(i, 1, a_hi, a_lo, KT, MEM)
            pe.wait_ge(S["job_out"], 2 * PAIRS_MEM)
            for g in range(4):
                if g >= 2:
                    pe.wait_ge(S["v_trc"], g - 1)
                mt, half = g // 2, g % 2
                for k in range(4):
                    mm = pe.transpose(ps[:, 6 + g % 2, k * P:(k + 1) * P], vT[:, 4 * half + k, mt * P:(mt + 1) * P], ident)
                mm.then_inc(S["v_tr"], 1)

            with pe.Fori(0, HALVES) as hf:
                q0 = Q_IN + hf * PAIRS_IN
                pe.wait_ge(S["act_lo"], KT * (2 + hf))
                job(q0, 0, a_hi, a_lo, KT)
                stats(1 + hf)
                job(q0, 1, a_hi, a_lo, KT)
                with pe.Fori(1, PAIRS_IN) as i:
                    job(q0 + i, 0, a_hi, a_lo, KT)
                    job(q0 + i, 1, a_hi, a_lo, KT)

            pe.wait_ge(S["job_out"], 2 * Q_TAIL)

            def mixer(c, par, first):
                v_in = zin[par][:, 2, :, :]
                pe.wait_ge(S["lora_in"], 2 * c + 2)
                pe.wait_ge(S["ksq_done"], c + 1)
                if not first:
                    pe.wait_ge(S["sg_mx"], 2 * c)
                for lhs, rhs, done, free in ((wl, wd[par][:], "lw_ps", None), (al, ad[par][:], "la_ps", "sw_done"),
                                             (gl, gd[par][:], "lg_ps", "a_done")):
                    for hh in range(2):
                        if free:
                            pe.wait_ge(S[free], 2 * c + hh + 1)
                        met(pe)
                        for h in range(HG):
                            hd = HG * hh + h
                            mm = pe.matmul(ps[0:RN, 6 + hh, h * L:(h + 1) * L], lhs[:, hd * RN:(hd + 1) * RN], rhs,
                                           start=True, stop=True)
                        mm.then_inc(S[done], 1)
                if not first:
                    pe.wait_ge(S["sa_ev"], c)
                for m in range(4):
                    mm = pe.transpose(ps[:, 5, m * L:(m + 1) * L], sv[par][:, m, :], ident)
                mm.then_inc(S["sg_tr"], 1)
                pe.wait_ge(S["gate_done"], 2 * c + 2)
                met(pe)
                for h in range(RH):
                    mm = pe.matmul(ps[0:RH, 6, 0:L], kkc2[:, h, :], k_sq[:, h, :], start=(h == 0), stop=(h == RH - 1))
                mm.then_inc(S["kn_ps"], 1)
                pe.wait_ge(S["kn_rc"], c + 1)
                for hh in (1, 0):
                    met(pe)
                    for h in range(HG):
                        mm = pe.matmul(ps[0:RN, 6 + hh, h * L:(h + 1) * L], kkr[:, HG * hh + h, :], n8[:, 1, :], start=True, stop=True)
                    mm.then_inc(S["kb_ps"], 1)
                pe.wait_ge(S["rk_done"], c + 1)
                pe.wait_ge(S["kk_done"], 2 * c + 2)
                met(pe)
                for h in range(RH):
                    mm = pe.matmul(ps[0:RH, 6, 0:L], rkc[:, h, :], rk[:, h, :], start=(h == 0), stop=(h == RH - 1))
                mm.then_inc(S["bon_ps"], 1)
                pe.wait_ge(S["bon_sb"], c + 1)
                for hh in range(2):
                    met(pe)
                    for h in range(HG):
                        mm = pe.matmul(ps[0:RN, 6 + hh, h * L:(h + 1) * L], hr[:, HG * hh + h, :], n8[:, 3, :], start=True, stop=True)
                    mm.then_inc(S["bonb_ps"], 1)
                pe.wait_ge(S["bon_v"], 2 * c + 2)
                for src, done, bank, need in ((v_in, "vtr", 7, None), (kt[par][:], "ktr", 6, "kt_done"),
                                              (bt[par][:], "btr", 7, "bt_done")):
                    if need:
                        pe.wait_ge(S[need], c + 1)
                    if done == "btr":
                        pe.wait_ge(S["vtc"], c + 1)
                    met(pe)
                    for h in range(RH):
                        mm = pe.transpose(ps[:, bank, h * RN:(h + 1) * RN], src[:, h, :], ident[0:RN, 0:RN])
                    mm.then_inc(S[done], 1)
                pe.wait_ge(S["qq_done"], c + 1)
                pe.wait_ge(S["rr_done"], c + 1)
                if not first:
                    pe.wait_ge(S["yc_sq"], 2 * c)
                    pe.wait_ge(S["yn_done"], 2 * c)
                    pe.wait_ge(S["yv_rt"], c)
                pe.wait_ge(S["sg_vh"], c + 1)
                for g in range(2):
                    if g:
                        pe.wait_ge(S["ev_sc"], 12 * c + 6)
                    for src, bank, done in ((bt, 0, "sc_b"), (kt, 2, "sc_k")):
                        met(pe)
                        for h in range(HG):
                            mm = pe.matmul(ps[:, bank + h // 2, (h % 2) * 2 * L:(h % 2 + 1) * 2 * L], src[par][:, g * HG + h, :],
                                           qr[par][:, g * HG + h, :, :], start=True, stop=True)
                        mm.then_inc(S[done], 1)
                    met(pe)
                    for h in range(HG):
                        mm = pe.matmul(ps[:, 4 + g, h * L:(h + 1) * L], qr[par][:, g * HG + h, 0, :], bt[par][:, g * HG + h, :],
                                       start=True, stop=True)
                    mm.then_inc(S["sc_a"], 1)
                for lv in range(1, len(LEVELS)):
                    b, nblk = LEVELS[lv], L // (2 * LEVELS[lv])
                    for g in range(2):
                        if lv == 1:
                            pe.wait_ge(S["ev_sc"], 12 * c + 12)
                        else:
                            pe.wait_ge(S["tu_ev"], 24 * c + 4 * (lv - 2) + 2 * g + 2)
                        met(pe)
                        for h in range(HG):
                            hd = g * HG + h
                            mm = pe.matmul(ps[:, g, h * RN:(h + 1) * RN], at[:, hd, :], left(tm, b, hd, 1), start=True, stop=True)
                        mm.then_inc(S["x_ps"], 1)
                    for g in range(2):
                        pe.wait_ge(S["x_ev"], 12 * c + 2 * (lv - 1) + g + 1)
                        met(pe)
                        for h in range(HG):
                            hd = g * HG + h
                            mm = pe.matmul(ps[:, 2 + g, h * RN:(h + 1) * RN], um[:, hd * L:(hd + 1) * L], left(xm, b, hd, 1),
                                           start=True, stop=True)
                        met(pe)
                        for h in range(HG):
                            hd = g * HG + h
                            mm = pe.matmul(ps[:, 2 + g, (HG + h) * RN:(HG + h + 1) * RN], xm[:, hd * L:(hd + 1) * L],
                                           right(um, b, hd, 1), start=True, stop=True)
                        mm.then_inc(S["tu_ps"], 1)
                pe.wait_ge(S["h0_done"], c + 1)
                pe.wait_ge(S["vtc"], c + 1)
                met(pe)
                for h in range(RH):
                    pe.matmul(ps[:, 4, h * RN:(h + 1) * RN], qr[par][:, h, 0, :], h_0[:, h, :], start=True, stop=False)
                    mm = pe.matmul(ps[:, 4, h * RN:(h + 1) * RN], qk[:, h, :], v_tok[par][:, h, :], start=False, stop=True)
                mm.then_inc(S["rhs_ps"], 1)
                pe.wait_ge(S["rhs_ev"], c + 1)
                pe.wait_ge(S["tu_ev"], 24 * c + 24)
                met(pe)
                for h in range(RH):
                    mm = pe.matmul(ps[:, 5, h * RN:(h + 1) * RN], um[:, h * L:(h + 1) * L], rhs_t[:, h, :], start=True, stop=True)
                mm.then_inc(S["sa_ps"], 1)
                pe.wait_ge(S["sa_ev"], c + 1)
                pe.wait_ge(S["ktc"], c + 1)
                pe.wait_ge(S["btc"], c + 1)
                met(pe)
                for h in range(RH):
                    pe.matmul(ps[0:RN, 4, h * RN:(h + 1) * RN], b_tok[par][:, h, :], sa_t[:, h, :], start=True, stop=False)
                    mm = pe.matmul(ps[0:RN, 4, h * RN:(h + 1) * RN], k_tok[par][:, h, :], v_tok[par][:, h, :], start=False, stop=True)
                mm.then_inc(S["h_ps"], 1)
                for hh in range(2):
                    met(pe)
                    for h in range(HG):
                        hd = HG * hh + h
                        o = ps[0:RN, hh, h * L:(h + 1) * L]
                        pe.matmul(o, sa_t[:, hd, :], rb[:, hd, :], start=True, stop=False)
                        pe.matmul(o, v_tok[par][:, hd, :], rkm[:, hd, :], start=False, stop=False)
                        mm = pe.matmul(o, h_0[:, hd, :], qr[par][:, hd, 1, :], start=False, stop=True)
                    mm.then_inc(S["y_ps"], 1)
                for hh in range(2):
                    pe.wait_ge(S["y_ev"], 2 * c + hh + 1)
                    met(pe)
                    mm = pe.matmul(ps[0:RN, 2 + hh, :], cent[:], y_raw[:, HG * hh:HG * hh + HG, :], start=True, stop=True)
                    mm.then_inc(S["yc_ps"], 1)
                pe.wait_ge(S["yc_sq"], 2 * c + 2)
                pe.wait_ge(S["h_add"], c + 1)
                met(pe)
                for h in range(RH):
                    mm = pe.matmul(ps[0:RH, 4, 0:L], hm[:, h, :], y_sq[:, h, :], start=(h == 0), stop=(h == RH - 1))
                mm.then_inc(S["yv_ps"], 1)
                pe.wait_ge(S["yv_rc"], c + 1)
                for hh in range(2):
                    met(pe)
                    for h in range(HG):
                        mm = pe.matmul(ps[0:RN, hh, h * L:(h + 1) * L], lnr[:, HG * hh + h, :], n8[:, 2, :], start=True, stop=True)
                    mm.then_inc(S["yb_ps"], 1)
                pe.wait_ge(S["sg_lb"], c + 1)
                for hh in range(2):
                    met(pe)
                    for h in range(HG):
                        g = HG * hh + h
                        mm = pe.matmul(ps[0:RN, 6 + hh, h * L:(h + 1) * L], v_lnb[:, g * RN:(g + 1) * RN], ws[:, g, :],
                                       start=True, stop=True)
                    mm.then_inc(S["sg_ps"], 1)
                pe.wait_ge(S["sg_mx"], 2 * c + 2)
                pe.sem_inc(S["end_pe"], 1)

            pe.wait_ge(S["rconst_done"], 11 + 3)
            mixer(0, 0, True)
            mixer(1, 1, False)
            with pe.Fori(1, CHUNKS // 2) as i:
                for par in range(2):
                    mixer(2 * i + par, par, False)

            pe.wait_ge(S["const_in"], 64)
            with pe.Fori(0, HALVES) as hf:
                q0 = Q_TAIL + hf * PAIRS_TAIL
                n0 = 1 + HALVES + 3 * hf
                lo0 = KT * (1 + HALVES) + 3 * KT * hf

                def phase(first_q, pairs, hi_in, lo_in, kn, stat=None):
                    job(first_q, 0, hi_in, lo_in, kn)
                    if stat is not None:
                        stats(stat)
                    job(first_q, 1, hi_in, lo_in, kn)
                    with pe.Fori(1, pairs) as i:
                        job(first_q + i, 0, hi_in, lo_in, kn)
                        job(first_q + i, 1, hi_in, lo_in, kn)

                pe.wait_ge(S["act_lo"], lo0 + KT)
                phase(q0, PAIRS_OUT, a_hi, a_lo, KT)
                pe.wait_ge(S["act_lo"], lo0 + 2 * KT)
                phase(q0 + PAIRS_OUT, PAIRS_OUT, b_hi, b_lo, KT, n0)
                pe.wait_ge(S["job_out"], 2 * (q0 + 2 * PAIRS_OUT))
                pe.wait_ge(S["kv_in"], 32 * (hf + 1))

                def scores(unit):
                    h, nb = unit // NB, unit % NB
                    if unit >= 2:
                        pe.wait_ge(S["s_exp"], 4 * (hf * 8 + unit - 1))
                    for t in range(4):
                        o = ps[:, 2 * (unit % 2) + t // 2, (t % 2) * MEM:(t % 2 + 1) * MEM]
                        for k in range(2):
                            mm = pe.matmul(o, q[:, 2 * h + k, nb * BANK + t * P:nb * BANK + (t + 1) * P], kT[:, 2 * h + k, :],
                                           start=(k == 0), stop=(k == 1))
                    mm.then_inc(S["s_ps"], 1)

                def turn(unit):
                    pe.wait_ge(S["s_nrm"], 4 * (hf * 8 + unit + 1))
                    if unit:
                        pe.wait_ge(S["p_ev"], hf * 8 + unit)
                    for mt in range(2):
                        for t in range(4):
                            mm = pe.transpose(ps[:, 4 + mt, t * P:(t + 1) * P], prob[:, unit % 2, t, mt * P:(mt + 1) * P], ident)
                    mm.then_inc(S["p_tr"], 1)

                def weigh(unit):
                    h = unit // NB
                    pe.wait_ge(S["p_ev"], hf * 8 + unit + 1)
                    if unit:
                        pe.wait_ge(S["o_hi"], hf * 8 + unit)
                        pe.wait_ge(S["o_lo"], hf * 8 + unit)
                    for k in range(2):
                        for mt in range(2):
                            mm = pe.matmul(ps[:, 6 + k, :], v[:, mt, (2 * h + k) * P:(2 * h + k + 1) * P], probT[:, unit % 2, mt, :],
                                           start=(mt == 0), stop=(mt == 1))
                    mm.then_inc(S["o_ps"], 1)

                scores(0)
                for unit in range(8):
                    if unit < 7:
                        scores(unit + 1)
                    turn(unit)
                    weigh(unit)
                pe.wait_ge(S["o_lo"], hf * 8 + 8)
                phase(q0 + 2 * PAIRS_OUT, PAIRS_OUT, b_hi, b_lo, KT)
                pe.wait_ge(S["act_lo"], lo0 + 3 * KT)
                at_q, f0 = 3 * PAIRS_OUT, 0
                for gi, n in enumerate(FF_GROUPS):
                    phase(q0 + at_q, n, a_hi, a_lo, KT, n0 + 1 if gi == 0 else None)
                    f0 += n
                    pe.wait_ge(S["prod_lo"], hf * FF_TILES + f0)
                    phase(q0 + at_q + n, PAIRS_OUT, b_hi, b_lo, n)
                    at_q += n + PAIRS_OUT
                stats(n0 + 2)

        @block.vector
        def _(dve):
            def root_to_rstd(n, cols=TB):
                dve.wait_ge(S["stat_rt"], n + 1)
                dve.reciprocal(rstd[:, 0:cols], rstd[:, 0:cols]).then_inc(S["rstd_done"], 1)
                dve.wait_ge(S["rstd_done"], n + 1)
                met(dve)

            dve.wait_ge(S["const_in"], 48)
            for k in range(KT):
                dve.wait_ge(S["act_hi"], k + 1)
                dve.scalar_tensor_tensor(a_lo[:, k, 0:MEM], mem_raw[:, k, :], gain[:, G_MEM, k:k + 1],
                                         a_hi[:, k, 0:MEM].bitcast(F32), ALU.mult, ALU.subtract).then_inc(S["act_lo"], 1)
            root_to_rstd(0, MEM)
            for half, dst in ((0, kT0), (1, vT)):
                with dve.Fori(0, KT // 2) as i:
                    for u in range(2):
                        dve.wait_ge(S["job_done"], half * KT + 2 * i + u + 1)
                        dve.tensor_tensor(dst[:, ds(2 * i + u, 1), :], slot(u)[:, 0:1, 0:MEM], rstd[:, 0:MEM].unsqueeze(1), ALU.mult
                                          ).then_inc(S["job_out"], 1)
            dve.wait_ge(S["job_out"], 2 * PAIRS_MEM)
            dve.sem_inc(S["kv_done"], 8)
            for g in range(4):
                mt, half = g // 2, g % 2
                dve.wait_ge(S["v_tr"], g + 1)
                dve.tensor_copy(v0[:, mt, half * BANK:(half + 1) * BANK], ps[:, 6 + g % 2, :]).then_inc(S["v_trc"], 1)
            dve.wait_ge(S["v_trc"], 4)
            dve.sem_inc(S["half_end"], 1)

            with dve.Fori(0, HALVES) as hf:
                q0 = Q_IN + hf * PAIRS_IN
                for k in range(KT):
                    dve.wait_ge(S["act_hi"], KT * (1 + hf) + k + 1)
                    dve.scalar_tensor_tensor(a_lo[:, k, :], in_raw[:, k, :], gain[:, G_IN, k:k + 1],
                                             a_hi[:, k, :].bitcast(F32), ALU.mult, ALU.subtract).then_inc(S["act_lo"], 1)
                root_to_rstd(1 + hf)

                def z_tile(i, u, shift):
                    m = 2 * i + u
                    done = hf * IN_TILES + m
                    dve.wait_ge(S["job_done"], 2 * (q0 + i) + u + 1)
                    dve.tensor_tensor(z_ext[:, u, 1:TB + 1], flat(slot(u)), rstd[:], ALU.mult).then_inc(S["job_out"], 1)
                    if not shift:
                        dve.wait_ge(S["job_out"], 2 * (q0 + i) + u + 1)
                        dve.sem_inc(S["z_ext_done"], 1)
                        return
                    k = m
                    met(dve)
                    dve.tensor_copy(z_ext[:, u, 0:1], carry[:, ds(k, 1)]).then_inc(S["z_ext_done"], 1)
                    dve.wait_ge(S["job_out"], 2 * (q0 + i) + u + 1)
                    dve.wait_ge(S["z_ext_done"], done + 1)
                    met(dve)
                    dve.tensor_copy(carry[:, ds(k, 1)], z_ext[:, u, TB:TB + 1]).then_inc(S["carry_done"], 1)
                    dve.tensor_tensor(work[:, u, :], z_ext[:, u, 0:TB], z_ext[:, u, 1:TB + 1], ALU.subtract
                                      ).then_inc(S["z_dif_done"], 1)
                    dve.wait_ge(S["z_dif_done"], hf * SHIFT_TILES + m + 1)
                    dve.wait_ge(S["carry_done"], hf * SHIFT_TILES + m + 1)
                    dve.wait_ge(S[f"z_st{u}"], 16 * (1 + hf * PAIRS_IN + i))
                    dve.scalar_tensor_tensor(z_out[:, u, :], work[:, u, :], mu[:, ds(k, 1)], z_ext[:, u, 1:TB + 1],
                                             ALU.mult, ALU.add).then_inc(S["z_out_done"], 1)
                    dve.wait_ge(S["z_out_done"], done + 1)

                dve.wait_ge(S["zero_done"], 4)
                with dve.Fori(0, SHIFT_TILES // 2) as i:
                    for u in range(2):
                        z_tile(i, u, True)
                with dve.Fori(SHIFT_TILES // 2, PAIRS_IN) as i:
                    for u in range(2):
                        dve.wait_ge(S["z_out_done"], hf * IN_TILES + 2 * i + u - 1)
                        z_tile(i, u, False)
                dve.wait_ge(S["z_out_done"], (hf + 1) * IN_TILES)
                dve.sem_inc(S["half_end"], 1)

            dve.wait_ge(S["rconst"], 16 * 17)
            dve.tensor_copy(low[:].rearrange("p l s c -> p (l s c)"), low_in[:]).then_inc(S["masks_done"], 1)
            dve.tensor_copy(tri[:].rearrange("p s c -> p (s c)"), tri_in[:]).then_inc(S["masks_done"], 1)
            dve.wait_ge(S["masks_done"], 2)
            dve.wait_ge(S["rconst_done"], 11)
            dve.copy_predicated(ws[:], tri[:, 1, 0:L].unsqueeze(1).to_broadcast([P, RH, L]), wsr).then_inc(S["rconst_done"], 1)
            dve.tensor_tensor(kkc2[:], kkc[:], kkc[:], ALU.mult).then_inc(S["rconst_done"], 1)
            dve.tensor_scalar(hc[:, 1, :], hc[:, 0, :], -1.0, 1.0, ALU.mult, ALU.add).then_inc(S["rconst_done"], 1)
            dve.wait_ge(S["rconst_done"], 11 + 3)

            def mixer(c, par, first):
                k_in, v_in = zin[par][:, 1, :, :], zin[par][:, 2, :, :]
                dve.wait_ge(S["sg_tr"], c + 1)
                dve.bn_stats(bn[:, 0:6], ps[:, 5, :]).then_inc(S["sg_bn"], 1)
                dve.wait_ge(S["sg_bn"], c + 1)
                met(dve)
                dve.bn_aggr(bn[:, 6:8], bn[:, 0:6]).then_inc(S["sg_ag"], 1)
                dve.wait_ge(S["sw_done"], 2 * c + 2)
                dve.tensor_tensor_scan(cum[:].rearrange("p h t -> p (h t)"), reset[:], sig_w[:].rearrange("p h t -> p (h t)"),
                                       0.0, ALU.mult, ALU.add).then_inc(S["cum_done"], 1)
                dve.wait_ge(S["cum_done"], c + 1)
                if not first:
                    dve.wait_ge(S["rr_done"], c)
                    dve.wait_ge(S["wend_done"], c)
                dve.tensor_tensor(cum_c[:], cum[:], cum[:, :, RN - 1:RN].to_broadcast([RN, RH, L]), ALU.subtract
                                  ).then_inc(S["cumc_done"], 1)
                dve.wait_ge(S["a_done"], 2 * c + 2)
                if not first:
                    dve.wait_ge(S["ktr"], c)
                    dve.wait_ge(S["sc_k"], 2 * c)
                for h in range(RH):
                    dve.tensor_scalar(k_mix[:, h, :], a_t[:, h, :], hc[:, 0, h:h + 1], hc[:, 1, h:h + 1], ALU.mult, ALU.add
                                      ).then_inc(S["kmix_done"], 1)
                dve.wait_ge(S["sg_rt"], c + 1)
                dve.reciprocal(bn[:, 9:10], bn[:, 8:9]).then_inc(S["sg_rc"], 1)
                dve.wait_ge(S["kn_rt"], c + 1)
                dve.tensor_scalar(n8[:, 0, :], n8[:, 0, :], 1e-12, None, ALU.max).then_inc(S["kn_mx"], 1)
                dve.wait_ge(S["kn_mx"], c + 1)
                dve.reciprocal(n8[:, 1, :], n8[:, 0, :]).then_inc(S["kn_rc"], 1)
                dve.wait_ge(S["sg_rc"], c + 1)
                if not first:
                    dve.wait_ge(S["sg_ps"], 2 * c)
                dve.tensor_scalar(v_hat[:], ps[:, 5, :], bn[:, 6:7], bn[:, 9:10], ALU.subtract, ALU.mult).then_inc(S["sg_vh"], 1)
                if not first:
                    dve.wait_ge(S["bv_done"], c)
                for n, hh in enumerate((1, 0)):
                    dve.wait_ge(S["kb_ps"], 2 * c + n + 1)
                    dve.tensor_tensor(kk[:, HG * hh:HG * hh + HG, :], k_in[:, HG * hh:HG * hh + HG, :],
                                      ps[0:RN, 6 + hh, :].rearrange("p (h t) -> p h t", t=L), ALU.mult).then_inc(S["kk_done"], 1)
                dve.wait_ge(S["kk_done"], 2 * c + 2)
                dve.wait_ge(S["w_done"], 4 * c + 4)
                dve.scalar_tensor_tensor(qr[par][:, :, 0, :], kk[:], -1.0, w_exc[:], ALU.mult, ALU.mult).then_inc(S["qq_done"], 1)
                dve.wait_ge(S["bv_done"], c + 1)
                dve.tensor_tensor(bt[par][:], b_vec[:], w_neg[:], ALU.mult).then_inc(S["bt_done"], 1)
                for hh in range(2):
                    dve.wait_ge(S["bonb_ps"], 2 * c + hh + 1)
                    dve.tensor_tensor(bonus[par][:, HG * hh:HG * hh + HG, :], v_in[:, HG * hh:HG * hh + HG, :],
                                      ps[0:RN, 6 + hh, :].rearrange("p (h t) -> p h t", t=L), ALU.mult).then_inc(S["bon_v"], 1)
                if not first:
                    dve.wait_ge(S["h_new"], c)
                    dve.wait_ge(S["y_ps"], 2 * c)
                dve.tensor_tensor(h_0[:], h_st[:], w_mid[par][:].unsqueeze(2).to_broadcast([RN, RH, RN]), ALU.mult
                                  ).then_inc(S["h0_done"], 1)
                for g in range(2):
                    hs = slice(g * HG, (g + 1) * HG)
                    strict = tri[:, 0, :].rearrange("p (h t) -> p h t", t=L)
                    incl = tri[:, 1, :].rearrange("p (h t) -> p h t", t=L)
                    sb_ = ps[:, 0:2, :].rearrange("p a (h w t) -> p (a h) w t", w=2, t=L)
                    sk_ = ps[:, 2:4, :].rearrange("p a (h w t) -> p (a h) w t", w=2, t=L)
                    dve.wait_ge(S["sc_b"], 2 * c + g + 1)
                    met(dve)
                    dve.copy_predicated(at[:, hs, :], strict, sb_[:, :, 0, :]).then_inc(S["ev_sc"], 1)
                    met(dve)
                    dve.copy_predicated(rb[:, hs, :], incl, sb_[:, :, 1, :]).then_inc(S["ev_sc"], 1)
                    dve.wait_ge(S["id_done"], 4 * c + 4)
                    dve.wait_ge(S["ev_sc"], 12 * c + 6 * g + 1)
                    met(dve)
                    dve.copy_predicated(right(um, 1, g * HG, HG), low[:, 0, 1, :].unsqueeze(2),
                                        at[:].rearrange("p h (n two) -> p (h n) two", two=2)[:, g * HG * RN:(g + 1) * HG * RN, 1:2]
                                        ).then_inc(S["ev_sc"], 1)
                    dve.wait_ge(S["sc_k"], 2 * c + g + 1)
                    met(dve)
                    dve.copy_predicated(qk[:, hs, :], strict, sk_[:, :, 0, :]).then_inc(S["ev_sc"], 1)
                    met(dve)
                    dve.copy_predicated(rkm[:, hs, :], incl, sk_[:, :, 1, :]).then_inc(S["ev_sc"], 1)
                    dve.wait_ge(S["sc_a"], 2 * c + g + 1)
                    met(dve)
                    dve.copy_predicated(left(tm, 1, g * HG, HG), low[:, 0, 0, :].unsqueeze(2),
                                        ps[:, 4 + g, :].rearrange("p (n two) -> p n two", two=2)[:, :, 0:1]).then_inc(S["ev_sc"], 1)
                for lv in range(1, len(LEVELS)):
                    b = LEVELS[lv]
                    for g in range(2):
                        dve.wait_ge(S["tu_ps"], 12 * c + 2 * (lv - 1) + g + 1)
                        met(dve)
                        dve.copy_predicated(left(tm, b, g * HG, HG), low[:, lv, 0, :].rearrange("p (n b) -> p n b", b=b),
                                            ps[:, 2 + g, 0:HG * RN].rearrange("p (n b) -> p n b", b=b)).then_inc(S["tu_ev"], 1)
                        met(dve)
                        dve.copy_predicated(right(um, b, g * HG, HG), low[:, lv, 1, :].rearrange("p (n b) -> p n b", b=b),
                                            ps[:, 2 + g, HG * RN:].rearrange("p (n b) -> p n b", b=b)).then_inc(S["tu_ev"], 1)
                dve.wait_ge(S["rhs_ps"], c + 1)
                dve.tensor_copy(rhs_t[:].rearrange("p h r -> p (h r)"), ps[:, 4, :]).then_inc(S["rhs_ev"], 1)
                dve.wait_ge(S["h_ps"], c + 1)
                dve.tensor_tensor(h_st[:], h_0[:], ps[0:RN, 4, :].rearrange("p (h r) -> p h r", r=RN), ALU.add).then_inc(S["h_add"], 1)
                dve.wait_ge(S["h_add"], c + 1)
                dve.wait_ge(S["wend_done"], c + 1)
                dve.tensor_tensor(h_st[:], h_st[:], w_end[par][:].unsqueeze(2).to_broadcast([RN, RH, RN]), ALU.mult
                                  ).then_inc(S["h_new"], 1)
                dve.wait_ge(S["yv_rt"], c + 1)
                dve.reciprocal(n8[:, 2, :], n8[:, 2, :]).then_inc(S["yv_rc"], 1)
                dve.wait_ge(S["yc_cp"], 2 * c + 2)
                for hh in range(2):
                    dve.wait_ge(S["yb_ps"], 2 * c + hh + 1)
                    dve.tensor_tensor(y_n[:, HG * hh:HG * hh + HG, :], y_cen[:, HG * hh:HG * hh + HG, :],
                                      ps[0:RN, hh, :].rearrange("p (h t) -> p h t", t=L), ALU.mult).then_inc(S["yn_done"], 1)
                if not first:
                    dve.wait_ge(S["sg_st"], 16 * c)
                for hh in range(2):
                    dve.wait_ge(S["sg_ps"], 2 * c + hh + 1)
                    dve.tensor_tensor(s_mix[:, HG * hh:HG * hh + HG, :], bsp[:, HG * hh:HG * hh + HG, :],
                                      ps[0:RN, 6 + hh, :].rearrange("p (h t) -> p h t", t=L), ALU.add).then_inc(S["sg_mx"], 1)
                dve.wait_ge(S["sg_mx"], 2 * c + 2)
                dve.sem_inc(S["end_dve"], 1)

            mixer(0, 0, True)
            mixer(1, 1, False)
            with dve.Fori(1, CHUNKS // 2) as i:
                for par in range(2):
                    mixer(2 * i + par, par, False)

            for e in ("pool", "act", "pe"):
                dve.wait_ge(S["end_" + e], CHUNKS)
            dve.sem_inc(S["half_end"], 1)
            with dve.Fori(0, HALVES) as hf:
                q0 = Q_TAIL + hf * PAIRS_TAIL
                n0 = 1 + HALVES + 3 * hf
                hi0 = KT * (1 + HALVES) + 3 * KT * hf
                x0 = hf * 3 * KT
                dve.wait_ge(S["y_in"], 32 * (hf + 1))
                for k in range(KT):
                    dve.wait_ge(S["act_hi"], hi0 + k + 1)
                    dve.tensor_tensor(a_lo[:, k, :], in_raw[:, k, :], a_hi[:, k, :].bitcast(F32), ALU.subtract).then_inc(S["act_lo"], 1)

                def at_k(t, k):
                    return t[:, k:k + 1, :] if isinstance(k, int) else t[:, ds(k, 1), :]

                def add_x(pair, u, k, done):
                    dve.wait_ge(S["job_done"], 2 * pair + u + 1)
                    dve.tensor_tensor(at_k(x, k), flat(slot(u)).unsqueeze(1), at_k(x, k), ALU.add).then_inc(S["job_out"], 1)
                    if done:
                        dve.wait_ge(S["job_out"], 2 * pair + u + 1)
                        dve.sem_inc(S["x_new"], 1)

                def residual(n, first_q, hi_t, lo_t, g):
                    with dve.Fori(0, PAIRS_OUT) as i:
                        for u in range(2):
                            k = 2 * i + u
                            add_x(first_q + i, u, k, True)
                            dve.wait_ge(S["act_hi"], hi0 + (n + 1) * KT + k + 1)
                            dve.scalar_tensor_tensor(at_k(lo_t, k), at_k(x, k), gain[:, g, ds(k, 1)], at_k(hi_t, k).bitcast(F32),
                                                     ALU.mult, ALU.subtract).then_inc(S["act_lo"], 1)

                residual(0, q0, b_hi, b_lo, G_ATT)
                root_to_rstd(n0)
                with dve.Fori(0, PAIRS_OUT) as i:
                    for u in range(2):
                        dve.wait_ge(S["job_done"], 2 * (q0 + PAIRS_OUT + i) + u + 1)
                        dve.tensor_tensor(q[:, ds(2 * i + u, 1), :], flat(slot(u)).unsqueeze(1), rstd[:].unsqueeze(1), ALU.mult
                                          ).then_inc(S["job_out"], 1)

                def maxima(unit):
                    b0, c0 = 2 * (unit % 2), 4 * (unit % 2)
                    dve.wait_ge(S["s_ps"], hf * 8 + unit + 1)
                    dve.tensor_reduce(stat_m[:, c0:c0 + 4], ps[:, b0:b0 + 2, :].rearrange("p a (t m) -> p (a t) m", m=MEM),
                                      mybir.AxisListType.X, ALU.max).then_inc(S["s_max"], 1)
                    dve.wait_ge(S["s_max"], hf * 8 + unit + 1)
                    if unit >= 2:
                        dve.wait_ge(S["s_exp"], 4 * (hf * 8 + unit - 1))
                    dve.tensor_scalar(stat_n[:, c0:c0 + 4], stat_m[:, c0:c0 + 4], -float(XD) ** -0.5, None, ALU.mult
                                      ).then_inc(S["s_neg"], 1)

                def normalise(unit):
                    c0 = 4 * (unit % 2)
                    dve.wait_ge(S["s_exp"], 4 * (hf * 8 + unit + 1))
                    dve.reciprocal(stat_r[:, c0:c0 + 4], stat_s[:, c0:c0 + 4]).then_inc(S["s_rcp"], 1)
                    dve.wait_ge(S["s_rcp"], hf * 8 + unit + 1)
                    for t in range(4):
                        dve.tensor_scalar(prob[:, unit % 2, t, :], prob[:, unit % 2, t, :], stat_r[:, c0 + t:c0 + t + 1], None,
                                          ALU.mult).then_inc(S["s_nrm"], 1)

                def out_lo(unit):
                    h, nb = unit // NB, unit % NB
                    cols = slice(nb * BANK, (nb + 1) * BANK)
                    dve.wait_ge(S["o_hi"], hf * 8 + unit + 1)
                    dve.tensor_tensor(b_lo[:, 2 * h:2 * h + 2, cols], ps[:, 6:8, :], b_hi[:, 2 * h:2 * h + 2, cols].bitcast(F32),
                                      ALU.subtract).then_inc(S["o_lo"], 1)

                maxima(0)
                for unit in range(8):
                    normalise(unit)
                    if unit < 7:
                        maxima(unit + 1)
                    if unit:
                        out_lo(unit - 1)
                out_lo(7)
                residual(1, q0 + 2 * PAIRS_OUT, a_hi, a_lo, G_FF)
                root_to_rstd(n0 + 1)

                def gated(pair, f_all, f):
                    done = hf * FF_TILES + f_all
                    dve.wait_ge(S["job_done"], 2 * pair + 1)
                    dve.tensor_tensor(work[:, 0, :], flat(slot(0)), rstd[:], ALU.mult).then_inc(S["job_out"], 1)
                    dve.wait_ge(S["job_out"], 2 * pair + 1)
                    dve.sem_inc(S["gate_s"], 1)
                    dve.wait_ge(S["job_done"], 2 * pair + 2)
                    dve.tensor_tensor(sq[:], flat(slot(1)), rstd[:], ALU.mult).then_inc(S["job_out"], 1)
                    dve.wait_ge(S["job_out"], 2 * pair + 2)
                    dve.wait_ge(S["gate_a"], done + 1)
                    dve.tensor_tensor(work[:, 1, :], work[:, 0, :], sq[:], ALU.mult).then_inc(S["prod"], 1)
                    dve.wait_ge(S["prod_hi"], done + 1)
                    dve.tensor_tensor(at_k(b_lo, f), work[:, 1:2, :], at_k(b_hi, f).bitcast(F32), ALU.subtract).then_inc(S["prod_lo"], 1)
                    dve.wait_ge(S["prod_lo"], done + 1)

                at_q, f0 = 3 * PAIRS_OUT, 0
                for gi, n in enumerate(FF_GROUPS):
                    with dve.Fori(0, n) as i:
                        gated(q0 + at_q + i, f0 + i, i)
                    with dve.Fori(0, PAIRS_OUT) as i:
                        for u in range(2):
                            add_x(q0 + at_q + n + i, u, 2 * i + u, gi == len(FF_GROUPS) - 1)
                            if gi < len(FF_GROUPS) - 1:
                                dve.wait_ge(S["job_out"], 2 * (q0 + at_q + n + i) + u + 1)
                    at_q += n + PAIRS_OUT
                    f0 += n
                root_to_rstd(n0 + 2)
                with dve.Fori(0, KT // 2) as i:
                    for u in range(2):
                        k = 2 * i + u
                        if True:
                            dve.wait_ge(S[f"fin_st{u}"], 16 * (1 + hf * (KT // 2) + i))
                        dve.scalar_tensor_tensor(work[:, u:u + 1, :], x[:, ds(k, 1), :], gain[:, G_FINAL, ds(k, 1)],
                                                 rstd[:].unsqueeze(1), ALU.mult, ALU.mult).then_inc(S["fin"], 1)
                for u in range(2):
                    dve.wait_ge(S[f"fin_st{u}"], 16 * (1 + (hf + 1) * (KT // 2)))
                dve.sem_inc(S["half_end"], 1)


def kernel(x, mem, norm1_g, w_in, shift_mu, w0, w_lora_up, a0, a_lora_up, g_lora_up, k_k, k_a, r_k, lnx_w, lnx_b,
           sgu_ln_w, sgu_ln_b, w_spatial, b_spatial, w_out, norm2_g, mem_norm_g, wq_x, wk_x, wv_x, wo_x, norm3_g,
           w_gate, w_up, w_down, norm_f_g):
    import numpy as np
    import concourse.bacc as bacc
    from concourse.bass_utils import run_bass_kernel_spmd as run

    A = np.ascontiguousarray
    arrays = {}
    arrays["xT"] = A(np.asarray(x)[0].T).reshape(KT, P, T)
    arrays["memT"] = A(np.asarray(mem)[0].T).reshape(KT, P, MEM)
    col = lambda g: np.asarray(g).reshape(-1, P).T
    arrays["gains"] = A(np.stack([col(norm1_g[0]), col(norm2_g[0]), col(norm3_g[0]), col(norm_f_g), col(mem_norm_g[0])], 1))

    def tiles(w):
        w = np.asarray(w)
        return w.reshape(w.shape[0] // P, P, w.shape[1] // P, P).transpose(2, 1, 0, 3)

    gate_t, up_t, down_t = tiles(w_gate[0]), tiles(w_up[0]), tiles(w_down[0])
    rows = [tiles(wk_x[0]), tiles(wv_x[0]), tiles(w_in[0]), tiles(w_out[0]), tiles(wq_x[0]), tiles(wo_x[0])]
    f0 = 0
    for n in FF_GROUPS:
        pair = np.stack([gate_t[f0:f0 + n], up_t[f0:f0 + n]], 1)
        rows.append(pair.reshape(2 * n, P, KT, P))
        down = np.zeros((D // P, P, KT, P), np.float32)
        down[:, :, 0:n] = down_t[:, :, f0:f0 + n]
        rows.append(down)
        f0 += n
    weights = np.concatenate(rows, 0)
    arrays["weights"] = A(weights.reshape(weights.shape[0], P, KT * P))
    arrays["shift_mu"] = A(col(shift_mu[0]))
    arrays["w_lora"] = A(np.concatenate([w_lora_up[0], np.asarray(w0[0])[None]], 0))
    arrays["a_lora"] = A(np.concatenate([a_lora_up[0], np.asarray(a0[0])[None]], 0))
    arrays["g_lora"] = A(np.asarray(g_lora_up[0]))
    hcol = lambda g: np.asarray(g).reshape(RH, RN).T
    arrays["head_cols"] = A(np.stack([hcol(k_a[0]), np.zeros((RN, RH), np.float32), hcol(lnx_b[0])], 1))

    def on_rows(g):
        out = np.zeros((RH, RH, RN), np.float32)
        for h in range(RH):
            out[h, h] = np.asarray(g).reshape(RH, RN)[h]
        return out

    def on_cols(g):
        return A(on_rows(g).transpose(2, 0, 1))

    arrays["kk_rows"], arrays["lnx_rows"] = on_rows(k_k[0]), on_rows(lnx_w[0])
    arrays["kk_cols"], arrays["rk_cols"] = on_cols(k_k[0]), on_cols(r_k[0])
    arrays["w_spatialT"] = A(np.asarray(w_spatial[0]).transpose(2, 0, 1))
    arrays["b_spatial"] = A(np.asarray(b_spatial[0]))
    arrays["sgu_ln"] = A(np.stack([np.asarray(sgu_ln_w[0]), np.asarray(sgu_ln_b[0])]))
    f32 = np.float32
    arrays["consts"] = A(np.stack([np.eye(P, dtype=f32), np.ones((P, P), f32)], 1))
    arrays["cen"] = (np.eye(RN) - 1.0 / RN).astype(f32)
    arrays["head_rows"] = on_rows(np.ones((RH, RN), f32))
    arrays["head_mean"] = on_cols(np.full((RH, RN), 1.0 / RN, f32))
    reset = np.ones((RN, RH, L), f32)
    reset[:, :, 0] = 0
    arrays["scan_reset"] = reset.reshape(RN, RH * L)
    i = np.arange(L)
    low = np.zeros((P, len(LEVELS), 2, HG, RN), f32)
    for n, b in enumerate(LEVELS):
        same = (i[:, None] // (2 * b)) == (i[None, :] // (2 * b))
        is_left = (i // b) % 2 == 0
        low[:, n, 0] = (same & ~is_left[:, None])[:, is_left][:, None, :]
        low[:, n, 1] = (same & is_left[:, None])[:, ~is_left][:, None, :]
    arrays["lower_masks"] = low.reshape(P, len(LEVELS) * 2 * HG * RN)
    tri = np.stack([i[:, None] < i[None, :], i[:, None] <= i[None, :]], 1).astype(f32)
    arrays["tri_masks"] = A(np.repeat(tri[:, :, None, :], HG, 2)).reshape(P, 2 * HG * L)

    nc = bacc.Bacc("TRN2", target_bir_lowering=False, num_devices=1)
    ins = {}
    for name, a in arrays.items():
        dt = mybir.dt.from_np(a.dtype)
        ins[name] = nc.dram_tensor(f"in_{name}", a.shape, dt, kind="ExternalInput").ap()
    out = nc.dram_tensor("outT", (KT, P, T), F32, kind="ExternalOutput").ap()
    hybrid_block_kernel(nc, outT=out, **ins)
    r = run(nc, [{f"in_{k}": v for k, v in arrays.items()}], core_ids=[0])
    return A(r.results[0]["outT"].reshape(D, T).T)[None]
```

```python
import math
from contextlib import ExitStack

import concourse.bass as bass
from concourse import mybir

ALU = mybir.AluOpType
ACT = mybir.ActivationFunctionType
F32 = mybir.dt.float32
F32R = mybir.dt.float32r
U8 = mybir.dt.uint8
ds = bass.ds

P = 128
T = 2048
D = 1024
KT = D // P
TB = 1024
HALVES = T // TB
BANK = 512
NB = TB // BANK
MEM = 256
XH, XD = 4, 256
FF_TILES = 2816 // P
FF_GROUPS = (8, 8, 6)
assert sum(FF_GROUPS) == FF_TILES

RH, RN = 8, 64
HP = RH // 2
N_ONES, N_SET = 5, 8
L = 128
CHUNKS = T // L
HG = 4
LEVELS = (1, 2, 4, 8, 16, 32, 64)
DECAY = math.exp(-0.5)
SHIFT_TILES = 14
IN_TILES = 22
RMS_EPS, LN_EPS, LNX_EPS = 1e-6, 1e-5, 64e-5

PAIRS_MEM = 8
PAIRS_IN = IN_TILES // 2
PAIRS_OUT = 4
PAIRS_TAIL = 3 * PAIRS_OUT + FF_TILES + len(FF_GROUPS) * PAIRS_OUT
Q_IN = PAIRS_MEM
Q_TAIL = Q_IN + HALVES * PAIRS_IN
ROW_IN = 2 * PAIRS_MEM
ROW_TAIL = ROW_IN + IN_TILES

G_IN, G_ATT, G_FF, G_FINAL, G_MEM = range(5)




def hybrid_block_kernel(nc, xT, memT, gains, weights, shift_mu, w_lora, a_lora, g_lora, head_cols,
                        kk_rows, lnx_rows, kk_cols, rk_spread, w_spatialT, b_spatial, sgu_ln, consts, cen,
                        head_mean, scan_reset, block_masks, tri_masks, outT):
    with ExitStack() as ctx:
        base = (nc.sbuf_base + 63) // 64 * 64
        used = {}

        def place(name, shape, dt, off):
            size = 1
            for n in shape[1:]:
                size *= n
            size *= 1 if dt == U8 else 4
            used[name] = base + off + size
            return nc.alloc_sbuf_tensor_at(name, list(shape), dt, offset=base + off)

        sems = {}

        def sem(name):
            sems[name] = ctx.enter_context(nc.semaphore(name))
            return sems[name]

        KB = 1024
        OX, OA, OB, OW, OS = 0, 32 * KB, 96 * KB, 160 * KB, 184 * KB
        x = place("x", [P, KT, TB], F32, OX)
        a_hi = place("a_hi", [P, KT, TB], F32R, OA)
        a_lo = place("a_lo", [P, KT, TB], F32R, OA + 32 * KB)
        b_hi = place("b_hi", [P, KT, TB], F32R, OB)
        b_lo = place("b_lo", [P, KT, TB], F32R, OB + 32 * KB)
        w_raw = place("w_raw", [P, 2, KT, P], F32, OW)
        w_hi = place("w_hi", [P, 2, KT, P], F32R, OW + 8 * KB)
        w_lo = place("w_lo", [P, 2, KT, P], F32R, OW + 16 * KB)
        rstd = place("rstd", [P, TB], F32, OS)
        sumsq = place("sumsq", [P, TB], F32, OS + 4 * KB)
        sq = place("sq", [P, TB], F32, OS + 8 * KB)
        work = place("work", [P, 2, TB], F32, OS + 12 * KB)
        cst = place("cst", [P, 2, P], F32, OS + 20 * KB)
        gain = place("gain", [P, 5, KT], F32, OS + 21 * KB)
        mu = place("mu", [P, SHIFT_TILES], F32, OS + 21 * KB + 160)
        carry = place("carry", [P, SHIFT_TILES], F32, OS + 21 * KB + 224)
        stat_m = place("stat_m", [P, 2 * 4], F32, OS + 21 * KB + 288)
        stat_n = place("stat_n", [P, 2 * 4], F32, OS + 21 * KB + 320)
        stat_s = place("stat_s", [P, 2 * 4], F32, OS + 21 * KB + 352)
        stat_r = place("stat_r", [P, 2 * 4], F32, OS + 21 * KB + 384)
        eps = place("eps", [P, 4], F32, OS + 21 * KB + 416)
        ident, ones = cst[:, 0, :], cst[:, 1, :]
        in_raw = place("in_raw", [P, KT, TB], F32, OB)
        z_ext = place("z_ext", [P, 2, TB + 16], F32, OB + 32 * KB)
        z_out = place("z_out", [P, 2, TB], F32, OB + 32 * KB + 8320)
        Z_END = OB + 32 * KB + 8320 + 8192
        mem_raw = place("mem_raw", [P, KT, MEM], F32, OS + 12 * KB)
        vT = place("vT", [P, KT, MEM], F32, Z_END)
        mem_hi = place("mem_hi", [P, KT, MEM], F32R, OX + 16 * KB)
        mem_lo = place("mem_lo", [P, KT, MEM], F32R, OX + 24 * KB)
        y_in_raw = place("y_in_raw", [P, KT, TB], F32, OA + 32 * KB)
        q = place("q", [P, KT, TB], F32, OA)
        kT = place("kT", [P, KT, MEM], F32, OA + 32 * KB)
        v = place("v", [P, 2, D], F32, OA + 40 * KB)
        prob = place("prob", [P, 2, 4, MEM], F32, OA + 48 * KB)
        probT = place("probT", [P, 2, 2, BANK], F32, OA + 56 * KB)
        kT0 = place("kT0", [P, KT, MEM], F32, OX)
        v0 = place("v0", [P, 2, D], F32, OX + 8 * KB)

        zT = nc.dram_tensor("zT", [IN_TILES * 2, RN, T], F32, kind="Internal").ap()
        yT = nc.dram_tensor("yT", [16, RN, T], F32, kind="Internal").ap()
        kT_d = nc.dram_tensor("kT_d", [P, KT * MEM], F32, kind="Internal").ap()
        v_d = nc.dram_tensor("v_d", [P, 2 * D], F32, kind="Internal").ap()
        zT_t = zT.rearrange("(m two) r t -> m (two r) t", two=2)
        yT_t = yT.rearrange("(k two) r t -> (two r) k t", two=2)
        yT_m = yT.rearrange("(k two) r t -> k (two r) t", two=2)

        ps = ctx.enter_context(nc.psum_tensor("ps", [P, 8, BANK], F32))

        roff = [0]

        def rw(name, shape, dt=F32):
            size = 1
            for n in shape[1:]:
                size *= n
            size = size * (1 if dt == U8 else 4)
            t = place(name, shape, dt, roff[0])
            roff[0] += (size + 31) // 32 * 32
            assert roff[0] <= OS + 20 * KB, (name, roff[0])
            return t

        low_in = place("low_in", [P, len(LEVELS), RN], F32, Z_END)
        tri_in = place("tri_in", [P, 2, L], F32, Z_END + 4 * KB)
        wsr = place("wsr", [P, RH, L], F32, Z_END + 5 * KB)
        wl = rw("wl", [P, RH * RN])
        al = rw("al", [P, RH * RN])
        gl = rw("gl", [P, RH * RN])
        hc = rw("hc", [P, 3, HP])
        kkr = rw("kkr", [P, HP, P])
        lnr = rw("lnr", [P, HP, P])
        rkx = rw("rkx", [P, HP, P])
        kkc = rw("kkc", [P, HP, RH])
        kkc2 = rw("kkc2", [P, HP, RH])
        hm = rw("hm", [P, HP, RH])
        cent = rw("cent", [P, P])
        reset = rw("reset", [P, HP * L])
        low = rw("low", [P, len(LEVELS), HG * RN], U8)
        tri = rw("tri", [P, 2, HG * L], U8)
        ws = rw("ws", [P, RH, L])
        bsp = rw("bsp", [P, HP, L])
        sln = rw("sln", [P, 2, 4 * L])
        assert roff[0] <= 32 * KB, roff[0]
        zin = [rw(f"zin{i}", [P, 12, L]) for i in range(2)]
        suv = [rw(f"suv{i}", [P, 8, L]) for i in range(2)]
        wd = [rw(f"wd{i}", [P, L]) for i in range(2)]
        ad = [rw(f"ad{i}", [P, L]) for i in range(2)]
        gd = [rw(f"gd{i}", [P, L]) for i in range(2)]
        qr = [rw(f"qr{i}", [P, RH, 2, L]) for i in range(2)]
        v_tok = [rw(f"v_tok{i}", [P, RH * RN]) for i in range(2)]
        k_tok = [rw(f"k_tok{i}", [P, RH * RN]) for i in range(2)]
        b_tok = [rw(f"b_tok{i}", [P, RH * RN]) for i in range(2)]
        gate = [rw(f"gate{i}", [P, HP, L]) for i in range(2)]
        bonus = [rw(f"bonus{i}", [P, HP, L]) for i in range(2)]
        w_mid = [rw(f"w_mid{i}", [P, HP]) for i in range(2)]
        w_end = [rw(f"w_end{i}", [P, HP]) for i in range(2)]
        (sig_w, a_t, cum, cum_c, cum_e, w_inc, w_neg, w_exc, k_sq, kk, k_mix, k_new, rk, b_vec, bt, kt, bon_raw,
         y_raw, y_cen, y_sq, y_n, y_b, y_out, s_mix, s_out) = (
            rw(n, [P, HP, L]) for n in
            ("sig_w a_t cum cum_c cum_e w_inc w_neg w_exc k_sq kk k_mix k_new rk b_vec bt kt bon_raw "
             "y_raw y_cen y_sq y_n y_b y_out s_mix s_out").split())
        n8 = rw("n8", [P, 6, L])
        at = rw("at", [P, RH, L])
        rb = rw("rb", [P, RH, L])
        qk = rw("qk", [P, RH, L])
        rkm = rw("rkm", [P, RH, L])
        tm = rw("tm", [P, RH * L])
        um = rw("um", [P, RH * L])
        xm = rw("xm", [P, RH * L])
        rhs_t = rw("rhs_t", [P, RH, RN])
        sa_t = rw("sa_t", [P, RH, RN])
        h_st = rw("h_st", [P, HP, RN])
        h_0 = rw("h_0", [P, HP, RN])
        h_1 = rw("h_1", [P, HP, RN])
        v_hat = rw("v_hat", [P, 4 * L])
        v_ln = rw("v_ln", [P, 4 * L])
        v_lnb = rw("v_lnb", [P, 4 * L])
        bn = rw("bn", [P, 12])
        for n, end in used.items():
            assert end <= nc.sbuf_usable_end, (n, end)

        for n in ("const_in in0 in1 in2 in3 xr_in0 xr_in1 sqa_done ws_zero const_ready mixers_done w_raw0 w_raw1 w_hi_done w_lo_done job_done job_out act_in sq_done sumsq_done "
                  "stat_ps stat_rt rstd_done z_ext_done z_dif_done z_out_done z_st0 z_st1 carry_done zero_done "
                  "kv_done v_tr v_trc kv_store kv_in x_new act_hi act_lo gate_s gate_a prod "
                  "prod_hi prod_lo s_ps s_max s_neg s_exp s_rcp s_nrm p_tr p_ev o_ps o_hi o_lo fin fin_st0 fin_st1 "
                  "rconst rconst_done zin0 zin1 lora_in lw_ps la_ps lg_ps sw_done a_done gate_done ksq_done kn_ps kn_rt kn_mx kn_rc "
                  "kb_ps kk_done cum_done cumc_done cume_done wneg_done wexc_done winc_done wmid_done wend_done kmix_done knew_done kt_done bv_done "
                  "bt_done qq_done qq0_done rr_done rr0_done rk_done bon_ps  bon_v bonus_done vtr ktr btr vtc ktc btc "
                  "id_done sc_b sc_k ev_sc tr_ps tr_ev x_ps x_ev tu_ps tu_ev h0_done rhs_ps rhs_ev sa_ps sa_ev h_ps h_add h_new "
                  "y_ps y_ev yc_ps yc_cp yc_sq yv_ps yv_rt yv_rc yb_ps yn_done yb_done yo_done y_st "
                  "sg_tr sg_bn sg_ag sg_rt sg_rc sg_vh sg_lw sg_lb sg_ps sg_mx sg_out sg_st met_pe met_dve met_sp").split():
            sem(n)
        S = sems

        def slot(j):
            return ps[:, 2 * j:2 * j + 2, :]

        def flat(ap):
            return ap.rearrange("p a b -> p (a b)")

        def left(t, b, h0, n):
            return t[:, h0 * L:(h0 + n) * L].rearrange("p (n two b) -> p n two b", two=2, b=b)[:, :, 0, :]

        def right(t, b, h0, n):
            return t[:, h0 * L:(h0 + n) * L].rearrange("p (n two b) -> p n two b", two=2, b=b)[:, :, 1, :]

        def bank4(b):
            return ps[:, b, :].rearrange("p (m t) -> p m t", t=L)

        def pairs_of(t, which, e):
            return t[e * RN:(e + 1) * RN].rearrange("p (m e) w t -> p m e w t", e=2)[:, :, e, which, :]

        def used_before(n):
            return not isinstance(n, int) or n >= 2

        def met(eng):
            names = {mybir.EngineType.PE: "met_pe", mybir.EngineType.SP: "met_sp"}
            eng.sem_inc(S[names.get(eng.engine, "met_dve")], 1)

        block = ctx.enter_context(nc.Block())

        @block.sync
        def _(sp):
            def load_pair(pair, row, first=False):
                for u in range(2):
                    if not first:
                        sp.wait_ge(S["w_lo_done"], 2 * pair + u - 1)
                    sp.dma_start(w_raw[:, u:u + 1, :, :].rearrange("p a k m -> p a (k m)"),
                                 weights[ds(row + u, 1)].rearrange("a p n -> p a n")
                                 ).then_inc(S[f"w_raw{u}"], 16)

            for n in ("z_st0", "z_st1", "fin_st0", "fin_st1", "y_st"):
                sp.sem_inc(S[n], 16)
            for dst, src in ((cst, consts), (gain, gains), (mu, shift_mu)):
                sp.dma_start(dst[:], src).then_inc(S["const_in"], 16)
            sp.dma_start(mem_raw[:], memT.rearrange("k p t -> p k t")).then_inc(S["act_in"], 16)
            load_pair(0, 0, first=True)

            def load_x(hf, j):
                sp.dma_start(in_raw[:, 2 * j:2 * j + 2, :], xT[2 * j:2 * j + 2, :, hf * TB:(hf + 1) * TB].rearrange("k p t -> p k t")
                             ).then_inc(S[f"in{j}"], 16)

            load_x(0, 0)
            for i in range(1, 4):
                load_pair(i, 2 * i)
                load_x(0, i)
            with sp.Fori(4, PAIRS_MEM) as i:
                load_pair(i, 2 * i)
            load_pair(Q_IN, ROW_IN)
            sp.wait_ge(S["kv_done"], 8)
            sp.wait_ge(S["v_trc"], 4)
            sp.dma_start(kT_d, kT0[:].rearrange("p k t -> p (k t)")).then_inc(S["kv_store"], 16)
            sp.dma_start(v_d, v0[:].rearrange("p k t -> p (k t)")).then_inc(S["kv_store"], 16)

            for hf in range(HALVES):
                def store_z(i):
                    for u in range(2):
                        sp.wait_ge(S["z_out_done"], hf * IN_TILES + 2 * i + u + 1)
                        sp.dma_start(zT_t[ds(2 * i + u, 1), :, hf * TB:(hf + 1) * TB].rearrange("a p t -> p a t"),
                                     z_out[:, u:u + 1, :]).then_inc(S[f"z_st{u}"], 16)

                def load_and_store(first, end):
                    with sp.Fori(first, end) as i:
                        load_pair(Q_IN + hf * PAIRS_IN + i, ROW_IN + 2 * i)
                        store_z(i - 1)

                load_and_store(1, 4)
                if hf == 0:
                    sp.wait_ge(S["act_lo"], 2 * KT)
                    sp.wait_ge(S["sumsq_done"], 2 * KT)
                    for j in range(4):
                        load_x(1, j)
                    load_and_store(4, 6)
                    sp.wait_ge(S["kv_store"], 32)
                    for dst, src in ((wl, w_lora), (al, a_lora), (gl, g_lora), (hc, head_cols), (kkr, kk_rows), (lnr, lnx_rows),
                                     (rkx, rk_spread), (kkc, kk_cols), (hm, head_mean), (cent, cen),
                                     (reset, scan_reset), (low_in, block_masks), (tri_in, tri_masks), (wsr, w_spatialT)):
                        sp.dma_start(dst[:], src).then_inc(S["rconst"], 16)
                    for e in range(2):
                        sp.dma_start(bsp[e * RN:(e + 1) * RN, :, :], b_spatial[e].partition_broadcast(RN)).then_inc(S["rconst"], 16)
                    sp.dma_start(sln[:], sgu_ln.partition_broadcast(P)).then_inc(S["rconst"], 16)
                    load_and_store(6, PAIRS_IN)
                    load_pair(Q_IN + PAIRS_IN, ROW_IN)
                else:
                    load_and_store(4, PAIRS_IN)
                store_z(PAIRS_IN - 1)
            for u in range(2):
                sp.wait_ge(S[f"z_st{u}"], 16 * (1 + HALVES * PAIRS_IN))
            sp.wait_ge(S["job_out"], 2 * Q_TAIL)

            def load_chunk(n, par, first=False):
                if not first:
                    for done in ("sg_out", "rr_done", "bon_v", "vtr", "lg_ps", "sg_tr", "ksq_done"):
                        sp.wait_ge(S[done], n - 1)
                at_n = ds(n * L, L)
                for dst, src in ((zin[par][:], zT_t[0:12, :, at_n].rearrange("m p t -> p m t")),
                                 (wd[par][0:RN, :], zT[24, :, at_n]),
                                 (ad[par][0:RN, :], zT[25, :, at_n]),
                                 (gd[par][:], zT_t[13, :, at_n]),
                                 (suv[par][:], zT_t[14:22, :, at_n].rearrange("m p t -> p m t"))):
                    sp.dma_start(dst, src).then_inc(S[f"zin{par}"], 16)

            def store_s(n):
                sp.wait_ge(S["sg_out"], n + 1)
                sp.dma_start(yT_m[HP:2 * HP, :, ds(n * L, L)].rearrange("m p t -> p m t"), s_out[:]).then_inc(S["sg_st"], 16)

            def store_y(n):
                sp.wait_ge(S["yo_done"], n + 1)
                met(sp)
                sp.dma_start(yT_m[0:HP, :, ds(n * L, L)].rearrange("m p t -> p m t"), y_out[:]).then_inc(S["y_st"], 16)

            load_chunk(0, 0, True)
            load_chunk(1, 1, True)
            store_s(0)
            load_chunk(2, 0)
            store_s(1)
            with sp.Fori(0, CHUNKS // 2 - 2) as i:
                for par in (1, 0):
                    at = 2 * i + 2 - par
                    load_chunk(at + 2, par)
                    store_y(at - 1)
                    store_s(at + 1)
            load_chunk(CHUNKS - 1, 1)
            store_y(CHUNKS - 4)
            store_s(CHUNKS - 2)
            store_y(CHUNKS - 3)
            store_s(CHUNKS - 1)
            store_y(CHUNKS - 2)
            store_y(CHUNKS - 1)
            sp.wait_ge(S["y_st"], 16 * (CHUNKS + 1))
            sp.wait_ge(S["sg_st"], 16 * CHUNKS)

            sp.dma_start(cst[:], consts).then_inc(S["const_in"], 16)
            def load_y(hf, j):
                sp.dma_start(y_in_raw[:, 2 * j:2 * j + 2, :], yT_t[:, 2 * j:2 * j + 2, hf * TB:(hf + 1) * TB]
                             ).then_inc(S[f"in{j}"], 16)

            def load_residual(hf, i, u):
                k = 2 * i + u
                if isinstance(i, int):
                    if i:
                        sp.wait_ge(S[f"xr_in{u}"], 16 * i)
                    sp.dma_start(x[:, k:k + 1, :], xT[k:k + 1, :, hf * TB:(hf + 1) * TB].rearrange("k p t -> p k t")
                                 ).then_inc(S[f"xr_in{u}"], 16)
                else:
                    sp.wait_ge(S[f"xr_in{u}"], 16 * (hf * (KT // 2) + i))
                    sp.dma_start(x[:, ds(k, 1), :], xT[ds(k, 1), :, hf * TB:(hf + 1) * TB].rearrange("k p t -> p k t")
                                 ).then_inc(S[f"xr_in{u}"], 16)

            sp.wait_ge(S["mixers_done"], 1)
            load_y(0, 0)
            load_pair(Q_TAIL, ROW_TAIL)
            for j in range(1, 4):
                load_y(0, j)
            load_residual(0, 0, 0)
            load_residual(0, 0, 1)
            load_pair(Q_TAIL + 1, ROW_TAIL + 2)
            for k in range(2, KT):
                load_residual(0, k // 2, k % 2)
            for hf in range(HALVES):
                base_q = Q_TAIL + hf * PAIRS_TAIL
                with sp.Fori(2, 2 * PAIRS_OUT) as i:
                    load_pair(base_q + i, ROW_TAIL + 2 * i)
                sp.wait_ge(S["job_done"], 2 * (base_q + PAIRS_OUT))
                sp.dma_start(kT[:].rearrange("p k t -> p (k t)"), kT_d).then_inc(S["kv_in"], 16)
                sp.dma_start(v[:].rearrange("p k t -> p (k t)"), v_d).then_inc(S["kv_in"], 16)
                with sp.Fori(2 * PAIRS_OUT, PAIRS_TAIL - 2) as i:
                    load_pair(base_q + i, ROW_TAIL + 2 * i)
                if hf == 0:
                    sp.wait_ge(S["job_done"], 2 * (base_q + PAIRS_TAIL - PAIRS_OUT))
                    for j in range(4):
                        load_y(1, j)
                for i in range(PAIRS_TAIL - 2, PAIRS_TAIL):
                    load_pair(base_q + i, ROW_TAIL + 2 * i)
                if hf == 0:
                    for i in range(2):
                        load_pair(base_q + PAIRS_TAIL + i, ROW_TAIL + 2 * i)

                with sp.Fori(0, KT // 2) as i:
                    for u in range(2):
                        sp.wait_ge(S["fin"], hf * KT + 2 * i + u + 1)
                        sp.dma_start(outT[ds(2 * i + u, 1), :, hf * TB:(hf + 1) * TB].rearrange("k p t -> p k t"),
                                     work[:, u:u + 1, :]).then_inc(S[f"fin_st{u}"], 16)
                        if hf == 0:
                            load_residual(1, i, u)
            for u in range(2):
                sp.wait_ge(S[f"fin_st{u}"], 16 * (1 + HALVES * KT // 2))

        @block.gpsimd
        def _(pool):
            def split_pair(pair):
                for u in range(2):
                    split_job(pair, u)

            def split_job(pair, u):
                pool.wait_ge(S["w_hi_done"], 2 * pair + u + 1)
                pool.tensor_tensor(w_lo[:, u, :, :], w_raw[:, u, :, :], w_hi[:, u, :, :].bitcast(F32),
                                   ALU.subtract).then_inc(S["w_lo_done"], 1)

            def square_tile(src, count, first):
                if first:
                    pool.tensor_tensor(sumsq[:, 0:src.shape[-1]], src, src, ALU.mult).then_inc(S["sumsq_done"], 1)
                else:
                    pool.wait_ge(S["sumsq_done"], count[1])
                    pool.tensor_tensor(sq[:, 0:src.shape[-1]], src, src, ALU.mult).then_inc(S["sq_done"], 1)
                    pool.wait_ge(S["sq_done"], count[0])
                    pool.tensor_tensor(sumsq[:, 0:src.shape[-1]], sumsq[:, 0:src.shape[-1]], sq[:, 0:src.shape[-1]],
                                       ALU.add).then_inc(S["sumsq_done"], 1)

            pool.memset(carry[:], 0.0).then_inc(S["zero_done"], 1)
            pool.memset(eps[:, 0:1], RMS_EPS).then_inc(S["zero_done"], 1)
            pool.memset(eps[:, 1:2], LN_EPS).then_inc(S["zero_done"], 1)
            pool.memset(eps[:, 2:3], LNX_EPS).then_inc(S["zero_done"], 1)
            pool.wait_ge(S["act_in"], 16)
            square_tile(mem_raw[:, 0, :], None, True)
            for k in range(1, 5):
                square_tile(mem_raw[:, k, :], (k, k), False)
            split_pair(0)
            for k in range(5, KT):
                square_tile(mem_raw[:, k, :], (k, k), False)
            with pool.Fori(1, PAIRS_MEM + 4) as i:
                split_pair(i)
            for j in range(4):
                pool.wait_ge(S[f"in{j}"], 32)
            pool.wait_ge(S["stat_ps"], 2)
            square_tile(in_raw[:, 0, :], None, True)
            with pool.Fori(1, KT) as i:
                split_pair(Q_IN + 3 + i)
                square_tile(in_raw[:, ds(i, 1), :].rearrange("p a t -> p (a t)"), (KT - 1 + i, 2 * KT + i), False)
            pool.wait_ge(S["kv_store"], 32)
            pool.memset(ws[:], 0.0).then_inc(S["ws_zero"], 1)
            with pool.Fori(0, PAIRS_IN) as i:
                split_pair(Q_IN + PAIRS_IN + i)

            pool.wait_ge(S["job_out"], 2 * Q_TAIL)
            for u in range(2):
                pool.wait_ge(S[f"z_st{u}"], 16 * (1 + HALVES * PAIRS_IN))
            pool.wait_ge(S["const_ready"], 5)
            pool.wait_ge(S["carry_done"], HALVES * SHIFT_TILES)
            pool.memset(n8[:], 0.0).then_inc(S["rconst_done"], 1)
            pool.wait_ge(S["rconst_done"], 1)
            for t in (wd[0], ad[0], wd[1], ad[1]):
                pool.memset(t[RN:P, :], 1.0).then_inc(S["rconst_done"], 1)
            pool.wait_ge(S["rconst_done"], N_ONES)
            for t in (qr[0], h_st, qr[1]):
                pool.memset(t[:], 0.0).then_inc(S["rconst_done"], 1)
            pool.wait_ge(S["rconst_done"], N_SET)

            def finish(c, par):
                pool.wait_ge(S["yn_done"], c + 1)
                pool.wait_ge(S["bonus_done"], c + 1)
                pool.tensor_tensor(y_b[:], y_n[:], bonus[par][:], ALU.add).then_inc(S["yb_done"], 1)
                pool.wait_ge(S["yb_done"], c + 1)
                pool.wait_ge(S["gate_done"], c + 1)
                pool.wait_ge(S["y_st"], 16 * c + 16)
                pool.tensor_tensor(y_out[:], y_b[:], gate[par][:], ALU.mult).then_inc(S["yo_done"], 1)
                pool.wait_ge(S["yo_done"], c + 1)

            def prepare(n, par, first):
                r_in, k_in = zin[par][:, 0:4, :], zin[par][:, 4:8, :]
                if not first:
                    pool.wait_ge(S["wexc_done"], n)
                pool.wait_ge(S["cumc_done"], n + 1)
                pool.tensor_tensor(cum_e[:], cum_c[:], sig_w[:], ALU.subtract).then_inc(S["cume_done"], 1)
                pool.wait_ge(S["kmix_done"], 4 * n + 4)
                if not first:
                    pool.wait_ge(S["kt_done"], n)
                    pool.wait_ge(S["rk_done"], n)
                pool.tensor_tensor(k_new[:], k_in, k_mix[:], ALU.mult).then_inc(S["knew_done"], 1)
                pool.wait_ge(S["knew_done"], n + 1)
                if not first:
                    pool.wait_ge(S["bon_ps"], n)
                pool.tensor_tensor(rk[:], r_in, k_new[:], ALU.mult).then_inc(S["rk_done"], 1)
                pool.wait_ge(S["sg_vh"], n + 1)
                if not first:
                    pool.wait_ge(S["sg_lb"], n)
                pool.tensor_tensor(v_ln[:], v_hat[:], sln[:, 0, :], ALU.mult).then_inc(S["sg_lw"], 1)
                pool.wait_ge(S["sg_lw"], n + 1)
                if not first:
                    pool.wait_ge(S["sg_ps"], n)
                pool.tensor_tensor(v_lnb[:], v_ln[:], sln[:, 1, :], ALU.add).then_inc(S["sg_lb"], 1)
                pool.wait_ge(S["kk_done"], n + 1)
                if not first:
                    pool.wait_ge(S["bt_done"], n)
                pool.tensor_tensor(b_vec[:], kk[:], a_t[:], ALU.mult).then_inc(S["bv_done"], 1)
                pool.wait_ge(S["wneg_done"], n + 1)
                if not first:
                    pool.wait_ge(S["ktr"], n)
                    pool.wait_ge(S["sc_k"], 2 * n)
                pool.tensor_tensor(kt[:], k_new[:], w_neg[:], ALU.mult).then_inc(S["kt_done"], 1)
                pool.wait_ge(S["winc_done"], n + 1)
                if used_before(n):
                    pool.wait_ge(S["y_ps"], n - 1)
                pool.tensor_tensor(pairs_of(qr[par], 1, 0), r_in[0:RN], w_inc[0:RN], ALU.mult).then_inc(S["rr0_done"], 1)
                pool.wait_ge(S["kt_done"], n + 1)
                pool.wait_ge(S["rr0_done"], n + 1)
                pool.tensor_tensor(pairs_of(qr[par], 1, 1), r_in[RN:P], w_inc[RN:P], ALU.mult).then_inc(S["rr_done"], 1)
                pool.wait_ge(S["rr_done"], n + 1)
                if used_before(n):
                    finish(n - 2, par)
                pool.wait_ge(S["bon_v"], n + 1)
                if used_before(n):
                    pool.wait_ge(S["yb_done"], n - 1)
                pool.tensor_tensor(bonus[par][:], bon_raw[:], hc[:, 2, :].unsqueeze(2).to_broadcast([P, HP, L]),
                                   ALU.add).then_inc(S["bonus_done"], 1)
                pool.wait_ge(S["sg_mx"], n + 1)
                if not first:
                    pool.wait_ge(S["sg_st"], 16 * n)
                pool.tensor_tensor(s_out[:], s_mix[:], suv[par][:, 0:4, :], ALU.mult).then_inc(S["sg_out"], 1)

            prepare(0, 0, True)
            prepare(1, 1, False)
            with pool.Fori(1, CHUNKS // 2) as i:
                for par in range(2):
                    prepare(2 * i + par, par, False)
            finish(CHUNKS - 2, 0)
            finish(CHUNKS - 1, 1)

            norms = 1 + HALVES
            for hf in range(HALVES):
                base_q = Q_TAIL + hf * PAIRS_TAIL
                base_x = hf * 3 * KT
                done = norms + 3 * hf

                def squares(n, k, first=False):
                    pool.wait_ge(S["x_new"], base_x + n * KT + k + 1)
                    if first:
                        pool.wait_ge(S["stat_ps"], done + n)
                    square_tile(x[:, ds(k, 1), :] if not isinstance(k, int) else x[:, k:k + 1, :],
                                ((done + n - 1) * (KT - 1) + k, (done + n) * KT + k), first)

                def squares_phase(n, q0, q_next):
                    split_pair(q0 + 1)
                    squares(n, 0, True)
                    squares(n, 1)
                    with pool.Fori(2, PAIRS_OUT) as i:
                        split_pair(q0 + i)
                        squares(n, 2 * i - 2)
                        squares(n, 2 * i - 1)
                    if q_next is not None:
                        split_pair(q_next)
                    squares(n, KT - 2)
                    squares(n, KT - 1)

                if hf == 0:
                    split_pair(base_q)
                squares_phase(0, base_q, base_q + PAIRS_OUT)
                with pool.Fori(PAIRS_OUT + 1, 2 * PAIRS_OUT + 1) as i:
                    split_pair(base_q + i)
                squares_phase(1, base_q + 2 * PAIRS_OUT, base_q + 3 * PAIRS_OUT)
                with pool.Fori(3 * PAIRS_OUT + 1, PAIRS_TAIL - PAIRS_OUT + 1) as i:
                    split_pair(base_q + i)
                squares_phase(2, base_q + PAIRS_TAIL - PAIRS_OUT, None if hf else base_q + PAIRS_TAIL)

        @block.scalar
        def _(act):
            def hi(pair, u, first=False):
                act.wait_ge(S[f"w_raw{u}"], 16 * (pair + 1))
                if not first:
                    act.wait_ge(S["job_done"], 2 * pair + u - 1)
                act.activation(w_hi[:, u, :, :], w_raw[:, u, :, :], ACT.Copy).then_inc(S["w_hi_done"], 1)

            def split_rms(n, stat_cols=TB):
                act.wait_ge(S["stat_ps"], n + 1)
                act.activation(sq_rt(stat_cols), stat_psum(stat_cols), ACT.Sqrt, bias=eps[:, 0:1], scale=1.0 / D
                               ).then_inc(S["stat_rt"], 1)

            def sq_rt(cols):
                return rstd[:, 0:cols]

            def stat_psum(cols):
                return ps[:, 4:6, :].rearrange("p a b -> p (a b)")[:, 0:cols]

            act.wait_ge(S["zero_done"], 4)
            act.wait_ge(S["const_in"], 48)
            act.wait_ge(S["act_in"], 16)
            for k in range(KT):
                act.activation(mem_hi[:, k, :], mem_raw[:, k, :], ACT.Copy, scale=gain[:, G_MEM, k:k + 1]
                               ).then_inc(S["act_hi"], 1)
            hi(0, 0, True)
            hi(0, 1, True)
            split_rms(0, MEM)

            def split_square(k):
                act.wait_ge(S[f"in{k // 2}"], 16)
                act.activation(a_hi[:, k, :], in_raw[:, k, :], ACT.Copy, scale=gain[:, G_IN, k:k + 1]).then_inc(S["act_hi"], 1)
                if k >= 2:
                    act.wait_ge(S["sumsq_done"], KT + max(2, k - 1))
                act.activation(z_out[:, k % 2, :], in_raw[:, k, :], ACT.Square).then_inc(S["sqa_done"], 1)

            for i in range(1, PAIRS_MEM):
                hi(i, 0)
                hi(i, 1)
                split_square(i - 1)
            hi(Q_IN, 0)
            split_square(KT - 1)
            hi(Q_IN, 1)

            for hf in range(HALVES):
                q0 = Q_IN + hf * PAIRS_IN
                act.wait_ge(S["job_out"], 2 * q0)
                split_rms(1 + hf)
                with act.Fori(1, SHIFT_TILES // 2 + 1) as i:
                    hi(q0 + i, 0)
                    hi(q0 + i, 1)

                def gelu(i, u):
                    m = 2 * i + u
                    act.wait_ge(S["z_ext_done"], hf * IN_TILES + m + 1)
                    act.wait_ge(S[f"z_st{u}"], 16 * (1 + hf * PAIRS_IN + i))
                    act.activation(z_out[:, u, :], z_ext[:, u, 1:TB + 1], ACT.Gelu_apprx_tanh).then_inc(S["z_out_done"], 1)

                with act.Fori(SHIFT_TILES // 2 + 1, PAIRS_IN) as i:
                    for u in range(2):
                        hi(q0 + i, u)
                        gelu(i - 1, u)
                if hf == 0:
                    hi(q0 + PAIRS_IN, 0)
                    gelu(PAIRS_IN - 1, 0)
                    for j in range(4):
                        act.wait_ge(S[f"in{j}"], 32)
                    act.wait_ge(S["job_done"], 2 * (q0 + PAIRS_IN))
                    for k in range(KT):
                        act.activation(a_hi[:, k, :], in_raw[:, k, :], ACT.Copy, scale=gain[:, G_IN, k:k + 1]
                                       ).then_inc(S["act_hi"], 1)
                        if k == 0:
                            hi(q0 + PAIRS_IN, 1)
                else:
                    gelu(PAIRS_IN - 1, 0)
                gelu(PAIRS_IN - 1, 1)

            def evac_x(c, lv):
                for g in range(2):
                    act.wait_ge(S["x_ps"], 12 * c + 2 * lv - 2 + g + 1)
                    act.activation(left(xm, LEVELS[lv], g * HG, HG),
                                   ps[:, 2 + g, 0:HG * RN].rearrange("p (n b) -> p n b", b=LEVELS[lv]),
                                   ACT.Copy).then_inc(S["x_ev"], 1)

            def evac_t(c, lv):
                for g in range(2):
                    act.wait_ge(S["tr_ps"], 12 * c + 2 * lv - 2 + g + 1)
                    act.activation(left(tm, LEVELS[lv], g * HG, HG), left(ps[:, g, :], LEVELS[lv], 0, HG), ACT.Copy
                                   ).then_inc(S["tr_ev"], 1)

            def loras_in(n, par, loads, first=False):
                act.wait_ge(S[f"zin{par}"], 16 * 5 * loads)
                act.activation(wd[par][0:RN, :], wd[par][0:RN, :], ACT.Tanh).then_inc(S["lora_in"], 1)
                act.activation(gd[par][:], gd[par][:], ACT.Sigmoid).then_inc(S["lora_in"], 1)
                if not first:
                    act.wait_ge(S["kn_ps"], n)
                act.activation(k_sq[:], zin[par][:, 4:8, :], ACT.Square).then_inc(S["ksq_done"], 1)

            def decays(n, first=False):
                act.wait_ge(S["lw_ps"], n + 1)
                if not first:
                    act.wait_ge(S["cume_done"], n)
                act.activation(sig_w[:], bank4(6), ACT.Sigmoid).then_inc(S["sw_done"], 1)

            def rates(n, first=False):
                act.wait_ge(S["la_ps"], n + 1)
                if not first:
                    act.wait_ge(S["bv_done"], n)
                act.activation(a_t[:], bank4(7), ACT.Sigmoid).then_inc(S["a_done"], 1)

            def gates(n, par):
                act.wait_ge(S["lg_ps"], n + 1)
                if used_before(n):
                    act.wait_ge(S["yo_done"], n - 1)
                act.activation(gate[par][:], bank4(6), ACT.Copy).then_inc(S["gate_done"], 1)

            def roots(n):
                act.wait_ge(S["kn_ps"], n + 1)
                act.activation(n8[0:RH, 0, :], ps[0:RH, 6, 0:L], ACT.Sqrt).then_inc(S["kn_rt"], 1)
                act.wait_ge(S["sg_ag"], n + 1)
                act.activation(bn[:, 8:9], bn[:, 7:8], ACT.Sqrt, bias=eps[:, 1:2]).then_inc(S["sg_rt"], 1)

            def exps_out(n, first=False):
                act.wait_ge(S["cume_done"], n + 1)
                if not first:
                    act.wait_ge(S["bt_done"], n)
                    act.wait_ge(S["kt_done"], n)
                    act.wait_ge(S["qq_done"], n)
                act.activation(w_neg[:], cum_c[:], ACT.Exp, scale=DECAY).then_inc(S["wneg_done"], 1)
                act.activation(w_exc[:], cum_e[:], ACT.Exp, scale=-DECAY).then_inc(S["wexc_done"], 1)

            def exps_in(n, par, first=False):
                if not first:
                    act.wait_ge(S["rr_done"], n)
                    act.wait_ge(S["rr0_done"], n)
                if used_before(n):
                    act.wait_ge(S["h_new"], n - 1)
                act.activation(w_inc[:], cum_c[:], ACT.Exp, scale=-DECAY).then_inc(S["winc_done"], 1)
                act.activation(w_mid[par][:], cum[:, :, RN - 1], ACT.Exp, scale=-DECAY).then_inc(S["wmid_done"], 1)
                act.activation(w_end[par][:], cum_c[:, :, L - 1], ACT.Exp, scale=-DECAY).then_inc(S["wend_done"], 1)

            def token_major(n, dst, tr, done, bank):
                act.wait_ge(S[tr], n + 1)
                act.activation(dst[:], ps[:, bank, :], ACT.Copy).then_inc(S[done], 1)

            def identities():
                for g in range(2):
                    act.activation(um[:, g * HG * L:(g + 1) * HG * L].rearrange("p (h t) -> p h t", t=L),
                                   ident.unsqueeze(1).to_broadcast([P, HG, L]), ACT.Copy).then_inc(S["id_done"], 1)

            def centred(c):
                act.wait_ge(S["yc_ps"], c + 1)
                act.activation(y_sq[:], bank4(4), ACT.Square).then_inc(S["yc_sq"], 1)
                act.activation(y_cen[:], bank4(4), ACT.Copy).then_inc(S["yc_cp"], 1)

            def deviation(c):
                act.wait_ge(S["yv_ps"], c + 1)
                act.activation(n8[0:RH, 3, :], ps[0:RH, 5, 0:L], ACT.Sqrt, bias=eps[0:RH, 2:3]).then_inc(S["yv_rt"], 1)

            def body(c, par, loads=None, first=False, last=False):
                n, npar = c + 1, 1 - par
                if not last:
                    loras_in(n, npar, loads)
                token_major(c, b_tok[par], "btr", "btc", 6)
                if not last:
                    decays(n)
                evac_t(c, 1)
                if not last:
                    rates(n)
                evac_x(c, 1)
                evac_t(c, 2)
                evac_x(c, 2)
                if not first:
                    centred(c - 1)
                evac_t(c, 3)
                evac_x(c, 3)
                if not last:
                    roots(n)
                evac_t(c, 4)
                evac_x(c, 4)
                if not first:
                    deviation(c - 1)
                if not last:
                    exps_out(n)
                evac_t(c, 5)
                evac_x(c, 5)
                if not last:
                    exps_in(n, npar)
                evac_t(c, 6)
                evac_x(c, 6)
                act.wait_ge(S["sa_ps"], c + 1)
                if not first:
                    act.wait_ge(S["y_ps"], c)
                act.activation(sa_t[:].rearrange("p h r -> p (h r)"), ps[:, 5, :], ACT.Copy).then_inc(S["sa_ev"], 1)
                if not last:
                    gates(n, npar)
                    identities()
                act.wait_ge(S["y_ps"], c + 1)
                act.activation(y_raw[:], bank4(5), ACT.Copy).then_inc(S["y_ev"], 1)
                if not last:
                    token_major(n, v_tok[npar], "vtr", "vtc", 6)
                    token_major(n, k_tok[npar], "ktr", "ktc", 7)

            act.wait_ge(S["rconst_done"], N_ONES)
            loras_in(0, 0, 1, True)
            decays(0, True)
            rates(0, True)
            roots(0)
            exps_out(0, True)
            exps_in(0, 0, True)
            gates(0, 0)
            identities()
            token_major(0, v_tok[0], "vtr", "vtc", 6)
            token_major(0, k_tok[0], "ktr", "ktc", 7)
            body(0, 0, 1, first=True)
            with act.Fori(0, CHUNKS // 2 - 1) as i:
                body(2 * i + 1, 1, i + 2)
                body(2 * i + 2, 0, i + 2)
            body(CHUNKS - 1, 1, last=True)
            centred(CHUNKS - 1)
            deviation(CHUNKS - 1)

            act.wait_ge(S["const_in"], 64)
            def split_y(hf):
                for k in range(KT):
                    act.wait_ge(S[f"in{k // 2}"], 16 * (HALVES + hf + 1))
                    act.activation(a_hi[:, k, :], y_in_raw[:, k, :], ACT.Copy).then_inc(S["act_hi"], 1)
                    if k == 0 and hf == 0:
                        hi(Q_TAIL, 0)
                        hi(Q_TAIL, 1)

            split_y(0)
            for hf in range(HALVES):
                q0 = Q_TAIL + hf * PAIRS_TAIL
                n0 = 1 + HALVES + 3 * hf
                base_x = hf * 3 * KT

                def split_x(n, k, dst, g):
                    act.wait_ge(S["x_new"], base_x + n * KT + k + 1)
                    act.activation(dst[:, ds(k, 1), :] if not isinstance(k, int) else dst[:, k:k + 1, :],
                                   x[:, ds(k, 1), :] if not isinstance(k, int) else x[:, k:k + 1, :], ACT.Copy,
                                   scale=gain[:, g, ds(k, 1)] if not isinstance(k, int) else gain[:, g, k:k + 1]
                                   ).then_inc(S["act_hi"], 1)

                def residual_phase(n, first_q, dst, g):
                    with act.Fori(1, PAIRS_OUT) as i:
                        for u in range(2):
                            hi(first_q + i, u)
                            split_x(n, 2 * i - 2 + u, dst, g)
                    for u in range(2):
                        hi(first_q + PAIRS_OUT, u)
                        split_x(n, KT - 2 + u, dst, g)

                residual_phase(0, q0, b_hi, G_ATT)
                split_rms(n0)
                with act.Fori(1, PAIRS_OUT) as i:
                    for u in range(2):
                        hi(q0 + PAIRS_OUT + i, u)
                for u in range(2):
                    hi(q0 + 2 * PAIRS_OUT, u)
                def exps(unit):
                    for t in range(4):
                        c = 4 * (unit % 2) + t
                        act.wait_ge(S["s_neg"], hf * 8 + unit + 1)
                        if unit >= 2:
                            act.wait_ge(S["p_tr"], hf * 8 + unit - 1)
                            act.wait_ge(S["s_rcp"], hf * 8 + unit - 1)
                        act.activation(prob[:, unit % 2, t, :],
                                       ps[:, 2 * (unit % 2) + t // 2, (t % 2) * MEM:(t % 2 + 1) * MEM], ACT.Exp,
                                       bias=stat_n[:, c:c + 1], scale=float(XD) ** -0.5, accum_out=stat_s[:, c:c + 1]
                                       ).then_inc(S["s_exp"], 1)

                def probs_out(unit):
                    act.wait_ge(S["p_tr"], hf * 8 + unit + 1)
                    if unit >= 2:
                        act.wait_ge(S["o_ps"], hf * 8 + unit - 1)
                    act.activation(probT[:, unit % 2, :, :], ps[:, 4:6, :], ACT.Copy).then_inc(S["p_ev"], 1)

                def out_hi(unit):
                    h, nb = unit // NB, unit % NB
                    act.wait_ge(S["o_ps"], hf * 8 + unit + 1)
                    act.activation(b_hi[:, 2 * h:2 * h + 2, nb * BANK:(nb + 1) * BANK], ps[:, 6:8, :], ACT.Copy
                                   ).then_inc(S["o_hi"], 1)

                exps(0)
                exps(1)
                for unit in range(8):
                    probs_out(unit)
                    if unit < 6:
                        exps(unit + 2)
                    out_hi(unit)
                residual_phase(1, q0 + 2 * PAIRS_OUT, a_hi, G_FF)
                split_rms(n0 + 1)
                def product(f_all, f):
                    act.wait_ge(S["gate_s"], hf * FF_TILES + f_all + 1)
                    act.activation(work[:, 0, :], work[:, 0, :], ACT.Silu).then_inc(S["gate_a"], 1)
                    act.wait_ge(S["prod"], hf * FF_TILES + f_all + 1)
                    act.activation(b_hi[:, ds(f, 1), :] if not isinstance(f, int) else b_hi[:, f:f + 1, :],
                                   work[:, 1:2, :], ACT.Copy).then_inc(S["prod_hi"], 1)

                at_q, f0 = 3 * PAIRS_OUT, 0
                for gi, n in enumerate(FF_GROUPS):
                    with act.Fori(1, n) as i:
                        hi(q0 + at_q + i, 0)
                        hi(q0 + at_q + i, 1)
                        product(f0 + i - 1, i - 1)
                    last = gi == len(FF_GROUPS) - 1
                    hi(q0 + at_q + n, 0)
                    hi(q0 + at_q + n, 1)
                    product(f0 + n - 1, n - 1)
                    with act.Fori(1, PAIRS_OUT + (not last)) as i:
                        hi(q0 + at_q + n + i, 0)
                        hi(q0 + at_q + n + i, 1)
                    at_q += n + PAIRS_OUT
                    f0 += n
                if hf == 0:
                    split_y(1)
                    for u in range(2):
                        hi(q0 + PAIRS_TAIL, u)
                act.wait_ge(S["job_out"], 2 * (q0 + PAIRS_TAIL))
                split_rms(n0 + 2)

        @block.tensor
        def _(pe):
            def job(pair, u, hi_in, lo_in, kn, cols=TB, first=False, lo_wait=None):
                pe.wait_ge(S["w_lo_done"], 2 * pair + u + 1)
                if not first:
                    pe.wait_ge(S["job_out"], 2 * pair + u - 1)
                nbs = max(1, cols // BANK)
                w = min(cols, BANK)
                for k in range(kn):
                    if lo_wait is not None:
                        lo_wait(k)
                    for wt, rs in ((w_hi, (hi_in, lo_in)), (w_lo, (hi_in,))):
                        for nb in range(nbs):
                            for r in rs:
                                mm = pe.matmul(slot(u)[:, nb, 0:w], wt[:, u, k, :], r[:, k, nb * w:(nb + 1) * w],
                                               start=(k == 0 and r is hi_in and wt is w_hi),
                                               stop=(k == kn - 1 and wt is w_lo))
                mm.then_inc(S["job_done"], 1)

            def stats(n, cols=TB):
                pe.wait_ge(S["sumsq_done"], KT * (n + 1))
                for nb in range(max(1, cols // BANK)):
                    w = min(cols, BANK)
                    mm = pe.matmul(ps[:, 4 + nb, 0:w], ones, sumsq[:, nb * w:(nb + 1) * w], start=True, stop=True)
                mm.then_inc(S["stat_ps"], 1)

            def split(before):
                return lambda k: pe.wait_ge(S["act_lo"], before + k + 1)

            pe.wait_ge(S["const_in"], 48)
            job(0, 0, mem_hi, mem_lo, KT, MEM, True, split(0))
            job(0, 1, mem_hi, mem_lo, KT, MEM, True)
            stats(0, MEM)
            with pe.Fori(1, PAIRS_MEM) as i:
                job(i, 0, mem_hi, mem_lo, KT, MEM)
                job(i, 1, mem_hi, mem_lo, KT, MEM)
            pe.wait_ge(S["job_out"], 2 * PAIRS_MEM)
            for g in range(4):
                if g >= 2:
                    pe.wait_ge(S["v_trc"], g - 1)
                mt, half = g // 2, g % 2
                for k in range(4):
                    mm = pe.transpose(ps[:, 6 + g % 2, k * P:(k + 1) * P], vT[:, 4 * half + k, mt * P:(mt + 1) * P], ident)
                mm.then_inc(S["v_tr"], 1)

            for hf in range(HALVES):
                q0 = Q_IN + hf * PAIRS_IN
                job(q0, 0, a_hi, a_lo, KT, lo_wait=split(KT * (1 + hf)))
                stats(1 + hf)
                job(q0, 1, a_hi, a_lo, KT)
                with pe.Fori(1, PAIRS_IN) as i:
                    job(q0 + i, 0, a_hi, a_lo, KT)
                    job(q0 + i, 1, a_hi, a_lo, KT)

            pe.wait_ge(S["job_out"], 2 * Q_TAIL)

            def cols(bank, i):
                return ps[:, bank, i * L:(i + 1) * L]

            def low_rank(lhs, rhs, bank, done):
                for i in range(HP):
                    mm = pe.matmul(cols(bank, i), lhs[:, i * P:(i + 1) * P], rhs, start=True, stop=True)
                mm.then_inc(S[done], 1)

            def lora_w(n, par, first=False):
                pe.wait_ge(S["lora_in"], 2 * n + 2)
                if not first:
                    pe.wait_ge(S["btc"], n)
                met(pe)
                low_rank(wl, wd[par][:], 6, "lw_ps")

            def lora_a(n, par, first=False):
                if not first:
                    pe.wait_ge(S["ktc"], n)
                    met(pe)
                low_rank(al, ad[par][:], 7, "la_ps")

            def lora_g(n, par):
                pe.wait_ge(S["kk_done"], n + 1)
                met(pe)
                low_rank(gl, gd[par][:], 6, "lg_ps")

            def turn_gate(n, par):
                pe.wait_ge(S["a_done"], n + 1)
                met(pe)
                for m in range(4):
                    mm = pe.transpose(cols(7, m), suv[par][:, 4 + m, :], ident)
                mm.then_inc(S["sg_tr"], 1)

            def per_head(lhs, rhs, bank, done):
                for i in range(HP):
                    mm = pe.matmul(ps[0:RH, bank, 0:L], lhs[:, i, :], rhs[:, i, :], start=(i == 0), stop=(i == HP - 1))
                mm.then_inc(S[done], 1)

            def over_channels(lhs, row, bank, done):
                for i in range(HP):
                    mm = pe.matmul(cols(bank, i), lhs[:, i, :], n8[:, row, :], start=True, stop=True)
                mm.then_inc(S[done], 1)

            def key_norms(n):
                pe.wait_ge(S["sw_done"], n + 1)
                pe.wait_ge(S["ksq_done"], n + 1)
                met(pe)
                per_head(kkc2, k_sq, 6, "kn_ps")

            def key_scales(n):
                pe.wait_ge(S["kn_rc"], n + 1)
                pe.wait_ge(S["kn_rt"], n + 1)
                met(pe)
                over_channels(kkr, 1, 6, "kb_ps")

            def bonus_sums(n):
                pe.wait_ge(S["rk_done"], n + 1)
                pe.wait_ge(S["sg_vh"], n + 1)
                met(pe)
                for i in range(HP):
                    mm = pe.matmul(cols(7, i), rkx[:, i, :], rk[:, i, :], start=True, stop=True)
                mm.then_inc(S["bon_ps"], 1)

            def mix_gate(n):
                pe.wait_ge(S["sg_lb"], n + 1)
                pe.wait_ge(S["bon_v"], n + 1)
                met(pe)
                for h in range(RH):
                    rows = slice((h % 2) * RN, (h % 2 + 1) * RN)
                    mm = pe.matmul(ps[rows, 7, (h // 2) * L:(h // 2 + 1) * L], v_lnb[:, h * RN:(h + 1) * RN], ws[:, h, :],
                                   start=True, stop=True)
                mm.then_inc(S["sg_ps"], 1)

            def turn(n, src, need, bank, free, done):
                for name in (need, free):
                    if name:
                        pe.wait_ge(S[name], n + 1)
                met(pe)
                for i in range(HP):
                    mm = pe.transpose(cols(bank, i), src[:, i, :], ident)
                mm.then_inc(S[done], 1)

            def turn_v(n, par):
                turn(n, zin[par][:, 8:12, :], None, 6, "gate_done", "vtr")

            def turn_k(n, par):
                turn(n, kt, "kt_done", 7, "sg_mx", "ktr")

            def turn_b(n, par):
                turn(n, bt, "bt_done", 6, "vtc", "btr")

            def scores(c, par, g, first=False):
                if not g:
                    pe.wait_ge(S["qq_done"], c + 1)
                    pe.wait_ge(S["rr_done"], c + 1)
                    pe.wait_ge(S["rr0_done"], c + 1)
                    if not first:
                        pe.wait_ge(S["tu_ev"], 12 * c)
                    pe.wait_ge(S["bt_done"], c + 1)
                    pe.wait_ge(S["kt_done"], c + 1)
                for src, bank, done, taken in ((bt, 0, "sc_b", 2), (kt, 2, "sc_k", 5)):
                    if g:
                        pe.wait_ge(S["ev_sc"], 10 * c + taken)
                    met(pe)
                    for h in range(HG):
                        mm = pe.matmul(ps[:, bank + h // 2, (h % 2) * 2 * L:(h % 2 + 1) * 2 * L], src[:, (g * HG + h) // 2, :],
                                       qr[par][:, g * HG + h, :, :], start=True, stop=True)
                    mm.then_inc(S[done], 1)

            def turn_inverse(c, lv, *between):
                for g in range(2):
                    if lv == 1:
                        pe.wait_ge(S["ev_sc"], 10 * c + 7 + g)
                    else:
                        pe.wait_ge(S["tu_ev"], 12 * c + 2 * (lv - 2) + g + 1)
                    met(pe)
                    for h in range(HG):
                        hd = g * HG + h
                        mm = pe.transpose(cols(g, h), um[:, hd * L:(hd + 1) * L], ident)
                    mm.then_inc(S["tr_ps"], 1)
                    if not g:
                        for step, args in between:
                            step(*args)

            def level(c, lv):
                b = LEVELS[lv]
                if lv == 1:
                    pe.wait_ge(S["ev_sc"], 10 * c + 10)
                for g in range(2):
                    pe.wait_ge(S["tr_ev"], 12 * c + 2 * (lv - 1) + g + 1)
                    met(pe)
                    for h in range(HG):
                        hd = g * HG + h
                        mm = pe.matmul(ps[:, 2 + g, h * RN:(h + 1) * RN], at[:, hd, :], left(tm, b, hd, 1), start=True, stop=True)
                    mm.then_inc(S["x_ps"], 1)
                for g in range(2):
                    pe.wait_ge(S["x_ev"], 12 * c + 2 * (lv - 1) + g + 1)
                    met(pe)
                    for h in range(HG):
                        hd = g * HG + h
                        mm = pe.matmul(ps[:, 2 + g, (HG + h) * RN:(HG + h + 1) * RN], xm[:, hd * L:(hd + 1) * L],
                                       right(um, b, hd, 1), start=True, stop=True)
                    mm.then_inc(S["tu_ps"], 1)

            def centre(c):
                pe.wait_ge(S["y_ev"], c + 1)
                pe.wait_ge(S["h_add"], 2 * c + 2)
                met(pe)
                pe.matmul(bank4(4), cent[:], y_raw[:], start=True, stop=True).then_inc(S["yc_ps"], 1)

            def variance(c):
                pe.wait_ge(S["yc_sq"], c + 1)
                met(pe)
                per_head(hm, y_sq, 5, "yv_ps")

            def scale_back(c):
                pe.wait_ge(S["yv_rc"], c + 1)
                pe.wait_ge(S["yc_cp"], c + 1)
                met(pe)
                over_channels(lnr, 4, 4, "yb_ps")

            def body(c, par, first=False, last=False):
                n, npar = c + 1, 1 - par
                scores(c, par, 0, first)
                turn_b(c, par)
                scores(c, par, 1)
                if not last:
                    lora_w(n, npar)
                ahead, behind = not last, not first
                turn_inverse(c, 1, *[(lora_a, (n, npar))] * ahead)
                level(c, 1)
                turn_inverse(c, 2, *[(turn_gate, (n, npar))] * ahead)
                if behind:
                    centre(c - 1)
                level(c, 2)
                turn_inverse(c, 3, *[(key_norms, (n,))] * ahead)
                level(c, 3)
                turn_inverse(c, 4, *[(variance, (c - 1,))] * behind)
                level(c, 4)
                turn_inverse(c, 5, *[(key_scales, (n,))] * ahead)
                if ahead:
                    bonus_sums(n)
                level(c, 5)
                turn_inverse(c, 6, *[(scale_back, (c - 1,))] * behind)
                level(c, 6)
                if not first:
                    pe.wait_ge(S["yn_done"], c)
                pe.wait_ge(S["h0_done"], c + 1)
                met(pe)
                for h in range(RH):
                    o = ps[:, 4, h * RN:(h + 1) * RN]
                    pe.matmul(o, qr[par][:, h, 0, :], h_0[:, h // 2, :], start=True, stop=False)
                    mm = pe.matmul(o, qk[:, h, :], v_tok[par][:, h * RN:(h + 1) * RN], start=False, stop=True)
                mm.then_inc(S["rhs_ps"], 1)
                if not last:
                    lora_g(n, npar)
                pe.wait_ge(S["rhs_ev"], c + 1)
                pe.wait_ge(S["tu_ev"], 12 * c + 12)
                met(pe)
                for h in range(RH):
                    mm = pe.matmul(ps[:, 5, h * RN:(h + 1) * RN], um[:, h * L:(h + 1) * L], rhs_t[:, h, :], start=True, stop=True)
                mm.then_inc(S["sa_ps"], 1)
                if not last:
                    mix_gate(n)
                pe.wait_ge(S["sa_ev"], c + 1)
                met(pe)
                for i in range(HP):
                    pr = slice(i * P, (i + 1) * P)
                    pe.matmul(cols(4, i), b_tok[par][:, pr], sa_t[:, 2 * i:2 * i + 2, :], start=True, stop=False)
                    mm = pe.matmul(cols(4, i), k_tok[par][:, pr], v_tok[par][:, pr], start=False, stop=True)
                mm.then_inc(S["h_ps"], 1)
                for h in range(RH):
                    o = ps[(h % 2) * RN:(h % 2 + 1) * RN, 5, (h // 2) * L:(h // 2 + 1) * L]
                    pe.matmul(o, sa_t[:, h, :], rb[:, h, :], start=True, stop=False)
                    pe.matmul(o, v_tok[par][:, h * RN:(h + 1) * RN], rkm[:, h, :], start=False, stop=False)
                    mm = pe.matmul(o, h_0[:, h // 2, :], qr[par][:, h, 1, :], start=False, stop=True)
                mm.then_inc(S["y_ps"], 1)
                if not last:
                    turn_v(n, npar)
                    turn_k(n, npar)

            pe.wait_ge(S["rconst_done"], N_ONES)
            lora_w(0, 0, True)
            lora_a(0, 0, True)
            turn_gate(0, 0)
            key_norms(0)
            key_scales(0)
            bonus_sums(0)
            lora_g(0, 0)
            mix_gate(0)
            turn_v(0, 0)
            turn_k(0, 0)
            body(0, 0, first=True)
            with pe.Fori(0, CHUNKS // 2 - 1) as i:
                body(2 * i + 1, 1)
                body(2 * i + 2, 0)
            body(CHUNKS - 1, 1, last=True)
            pe.wait_ge(S["h_add"], 2 * CHUNKS)
            centre(CHUNKS - 1)
            variance(CHUNKS - 1)
            scale_back(CHUNKS - 1)
            pe.wait_ge(S["yn_done"], CHUNKS)

            pe.wait_ge(S["const_in"], 64)
            for hf in range(HALVES):
                q0 = Q_TAIL + hf * PAIRS_TAIL
                n0 = 1 + HALVES + 3 * hf
                lo0 = KT * (1 + HALVES) + 3 * KT * hf

                def phase(first_q, pairs, hi_in, lo_in, kn, stat=None, lo_wait=None):
                    job(first_q, 0, hi_in, lo_in, kn, lo_wait=lo_wait)
                    if stat is not None:
                        stats(stat)
                    job(first_q, 1, hi_in, lo_in, kn)
                    with pe.Fori(1, pairs) as i:
                        job(first_q + i, 0, hi_in, lo_in, kn)
                        job(first_q + i, 1, hi_in, lo_in, kn)

                phase(q0, PAIRS_OUT, a_hi, a_lo, KT, n0 - 1 if hf else None, split(lo0))
                phase(q0 + PAIRS_OUT, PAIRS_OUT, b_hi, b_lo, KT, n0, split(lo0 + KT))
                pe.wait_ge(S["kv_in"], 32 * (hf + 1))

                def scores(unit):
                    h, nb = unit // NB, unit % NB
                    if unit >= 2:
                        pe.wait_ge(S["s_exp"], 4 * (hf * 8 + unit - 1))
                    else:
                        pe.wait_ge(S["job_out"], 2 * (q0 + 2 * PAIRS_OUT) - 1 + unit)
                    for t in range(4):
                        o = ps[:, 2 * (unit % 2) + t // 2, (t % 2) * MEM:(t % 2 + 1) * MEM]
                        for k in range(2):
                            mm = pe.matmul(o, q[:, 2 * h + k, nb * BANK + t * P:nb * BANK + (t + 1) * P], kT[:, 2 * h + k, :],
                                           start=(k == 0), stop=(k == 1))
                    mm.then_inc(S["s_ps"], 1)

                def turn(unit):
                    pe.wait_ge(S["s_nrm"], 4 * (hf * 8 + unit + 1))
                    if unit:
                        pe.wait_ge(S["p_ev"], hf * 8 + unit)
                    for mt in range(2):
                        for t in range(4):
                            mm = pe.transpose(ps[:, 4 + mt, t * P:(t + 1) * P], prob[:, unit % 2, t, mt * P:(mt + 1) * P], ident)
                    mm.then_inc(S["p_tr"], 1)

                def weigh(unit):
                    h = unit // NB
                    pe.wait_ge(S["p_ev"], hf * 8 + unit + 1)
                    if unit:
                        pe.wait_ge(S["o_hi"], hf * 8 + unit)
                        pe.wait_ge(S["o_lo"], hf * 8 + unit)
                    for k in range(2):
                        for mt in range(2):
                            mm = pe.matmul(ps[:, 6 + k, :], v[:, mt, (2 * h + k) * P:(2 * h + k + 1) * P], probT[:, unit % 2, mt, :],
                                           start=(mt == 0), stop=(mt == 1))
                    mm.then_inc(S["o_ps"], 1)

                scores(0)
                scores(1)
                turn(0)
                for unit in range(8):
                    if unit < 6:
                        scores(unit + 2)
                    weigh(unit)
                    if unit < 7:
                        turn(unit + 1)
                phase(q0 + 2 * PAIRS_OUT, PAIRS_OUT, b_hi, b_lo, KT,
                      lo_wait=lambda k: pe.wait_ge(S["o_lo"], hf * 8 + 2 * (k // 2) + 2))
                at_q, f0 = 3 * PAIRS_OUT, 0
                for gi, n in enumerate(FF_GROUPS):
                    phase(q0 + at_q, n, a_hi, a_lo, KT, None if gi else n0 + 1, None if gi else split(lo0 + 2 * KT))
                    before = hf * FF_TILES + f0
                    phase(q0 + at_q + n, PAIRS_OUT, b_hi, b_lo, n,
                          lo_wait=lambda k: pe.wait_ge(S["prod_lo"], before + k + 1))
                    f0 += n
                    at_q += n + PAIRS_OUT
            stats(4 * HALVES)

        @block.vector
        def _(dve):
            def root_to_rstd(n, cols=TB):
                dve.wait_ge(S["stat_rt"], n + 1)
                dve.reciprocal(rstd[:, 0:cols], rstd[:, 0:cols]).then_inc(S["rstd_done"], 1)
                dve.wait_ge(S["rstd_done"], n + 1)
                met(dve)

            dve.wait_ge(S["const_in"], 48)
            for k in range(KT):
                dve.wait_ge(S["act_hi"], k + 1)
                dve.scalar_tensor_tensor(mem_lo[:, k, :], mem_raw[:, k, :], gain[:, G_MEM, k:k + 1],
                                         mem_hi[:, k, :].bitcast(F32), ALU.mult, ALU.subtract).then_inc(S["act_lo"], 1)
            root_to_rstd(0, MEM)

            def x_lo(hf, k):
                dve.wait_ge(S["act_hi"], KT * (1 + hf) + k + 1)
                dve.scalar_tensor_tensor(a_lo[:, k, :], in_raw[:, k, :], gain[:, G_IN, k:k + 1],
                                         a_hi[:, k, :].bitcast(F32), ALU.mult, ALU.subtract).then_inc(S["act_lo"], 1)

            for i in range(PAIRS_MEM):
                dst, k = (kT0, 2 * i) if i < KT // 2 else (vT, 2 * i - KT)
                for u in range(2):
                    dve.wait_ge(S["job_done"], 2 * i + u + 1)
                    dve.tensor_tensor(dst[:, k + u, :], slot(u)[:, 0, 0:MEM], rstd[:, 0:MEM], ALU.mult).then_inc(S["job_out"], 1)
                x_lo(0, i)
                if i:
                    dve.wait_ge(S["sqa_done"], i + 1)
                if i == 1:
                    dve.tensor_tensor(sumsq[:], z_out[:, 0, :], z_out[:, 1, :], ALU.add).then_inc(S["sumsq_done"], 2)
                elif i:
                    dve.wait_ge(S["sumsq_done"], KT + i)
                    dve.tensor_tensor(sumsq[:], sumsq[:], z_out[:, i % 2, :], ALU.add).then_inc(S["sumsq_done"], 1)
            dve.wait_ge(S["job_out"], 2 * PAIRS_MEM)
            dve.sem_inc(S["kv_done"], 8)
            for g in range(4):
                mt, half = g // 2, g % 2
                dve.wait_ge(S["v_tr"], g + 1)
                dve.tensor_copy(v0[:, mt, half * BANK:(half + 1) * BANK], ps[:, 6 + g % 2, :]).then_inc(S["v_trc"], 1)
            dve.wait_ge(S["v_trc"], 4)

            for hf in range(HALVES):
                q0 = Q_IN + hf * PAIRS_IN
                if hf:
                    for k in range(KT):
                        x_lo(hf, k)
                root_to_rstd(1 + hf)

                def z_tile(i, u, shift):
                    m = 2 * i + u
                    done = hf * IN_TILES + m
                    dve.wait_ge(S["job_done"], 2 * (q0 + i) + u + 1)
                    dve.tensor_tensor(z_ext[:, u, 1:TB + 1], flat(slot(u)), rstd[:], ALU.mult).then_inc(S["job_out"], 1)
                    if not shift:
                        dve.wait_ge(S["job_out"], 2 * (q0 + i) + u + 1)
                        dve.sem_inc(S["z_ext_done"], 1)
                        return
                    k = m
                    met(dve)
                    dve.tensor_copy(z_ext[:, u, 0:1], carry[:, ds(k, 1)]).then_inc(S["z_ext_done"], 1)
                    dve.wait_ge(S["job_out"], 2 * (q0 + i) + u + 1)
                    dve.wait_ge(S["z_ext_done"], done + 1)
                    met(dve)
                    dve.tensor_copy(carry[:, ds(k, 1)], z_ext[:, u, TB:TB + 1]).then_inc(S["carry_done"], 1)
                    dve.tensor_tensor(work[:, u, :], z_ext[:, u, 0:TB], z_ext[:, u, 1:TB + 1], ALU.subtract
                                      ).then_inc(S["z_dif_done"], 1)
                    dve.wait_ge(S["z_dif_done"], hf * SHIFT_TILES + m + 1)
                    dve.wait_ge(S["carry_done"], hf * SHIFT_TILES + m + 1)
                    dve.wait_ge(S[f"z_st{u}"], 16 * (1 + hf * PAIRS_IN + i))
                    dve.scalar_tensor_tensor(z_out[:, u, :], work[:, u, :], mu[:, ds(k, 1)], z_ext[:, u, 1:TB + 1],
                                             ALU.mult, ALU.add).then_inc(S["z_out_done"], 1)
                    dve.wait_ge(S["z_out_done"], done + 1)

                dve.wait_ge(S["zero_done"], 4)
                with dve.Fori(0, SHIFT_TILES // 2) as i:
                    for u in range(2):
                        z_tile(i, u, True)
                with dve.Fori(SHIFT_TILES // 2, PAIRS_IN) as i:
                    for u in range(2):
                        dve.wait_ge(S["z_out_done"], hf * IN_TILES + 2 * i + u - 1)
                        z_tile(i, u, False)
                if hf == 0:
                    dve.wait_ge(S["rconst"], 16 * 17)
                    dve.tensor_copy(low[:].rearrange("p l (h c) -> p l h c", c=RN),
                                    low_in[:].unsqueeze(2).to_broadcast([P, len(LEVELS), HG, RN])).then_inc(S["const_ready"], 1)
                    dve.tensor_copy(tri[:].rearrange("p s (h c) -> p s h c", c=L),
                                    tri_in[:].unsqueeze(2).to_broadcast([P, 2, HG, L])).then_inc(S["const_ready"], 1)
                    dve.wait_ge(S["const_ready"], 2)
                    dve.wait_ge(S["ws_zero"], 1)
                    dve.copy_predicated(ws[:], tri[:, 1, 0:L].unsqueeze(1).to_broadcast([P, RH, L]), wsr[:]
                                        ).then_inc(S["const_ready"], 1)
                    dve.tensor_tensor(kkc2[:], kkc[:], kkc[:], ALU.mult).then_inc(S["const_ready"], 1)
                    dve.tensor_scalar(hc[:, 1, :], hc[:, 0, :], -1.0, 1.0, ALU.mult, ALU.add).then_inc(S["const_ready"], 1)

            for u in range(2):
                dve.wait_ge(S[f"z_st{u}"], 16 * (1 + HALVES * PAIRS_IN))
            dve.wait_ge(S["job_out"], 2 * Q_TAIL)
            for t in (at, rb, qk, rkm, xm):
                dve.memset(t[:], 0.0).then_inc(S["const_ready"], 1)
            dve.wait_ge(S["const_ready"], 10)
            strict = tri[:, 0, :].rearrange("p (h t) -> p h t", t=L)
            inclusive = tri[:, 1, :].rearrange("p (h t) -> p h t", t=L)

            def take(out, mask, data, done):
                met(dve)
                dve.copy_predicated(out, mask, data).then_inc(S[done], 1)

            def take_scores(c, g):
                hs = slice(g * HG, (g + 1) * HG)
                by_b = ps[:, 0:2, :].rearrange("p a (h w t) -> p (a h) w t", w=2, t=L)
                by_k = ps[:, 2:4, :].rearrange("p a (h w t) -> p (a h) w t", w=2, t=L)
                dve.wait_ge(S["sc_b"], 2 * c + g + 1)
                take(at[:, hs, :], strict, by_b[:, :, 0, :], "ev_sc")
                take(rb[:, hs, :], inclusive, by_b[:, :, 1, :], "ev_sc")
                dve.wait_ge(S["id_done"], 2 * c + 2)
                dve.wait_ge(S["ev_sc"], 10 * c + 5 * g + 1)
                take(right(um, 1, g * HG, HG), low[:, 0, :].unsqueeze(2),
                     at[:].rearrange("p h (n two) -> p (h n) two", two=2)[:, g * HG * RN:(g + 1) * HG * RN, 1:2], "ev_sc")
                dve.wait_ge(S["sc_k"], 2 * c + g + 1)
                take(qk[:, hs, :], strict, by_k[:, :, 0, :], "ev_sc")
                take(rkm[:, hs, :], inclusive, by_k[:, :, 1, :], "ev_sc")

            def take_level(c, lv):
                b = LEVELS[lv]
                for g in range(2):
                    dve.wait_ge(S["tu_ps"], 12 * c + 2 * (lv - 1) + g + 1)
                    take(right(um, b, g * HG, HG), low[:, lv, :].rearrange("p (n b) -> p n b", b=b),
                         ps[:, 2 + g, HG * RN:].rearrange("p (n b) -> p n b", b=b), "tu_ev")

            def sum_decays(n, first=False):
                dve.wait_ge(S["sw_done"], n + 1)
                if not first:
                    dve.wait_ge(S["wmid_done"], n)
                dve.tensor_tensor_scan(cum[:].rearrange("p h t -> p (h t)"), reset[:], sig_w[:].rearrange("p h t -> p (h t)"),
                                       0.0, ALU.mult, ALU.add).then_inc(S["cum_done"], 1)
                dve.wait_ge(S["cum_done"], n + 1)
                if not first:
                    dve.wait_ge(S["wend_done"], n)
                dve.tensor_tensor(cum_c[:], cum[:], cum[:, :, RN - 1:RN].to_broadcast([P, HP, L]), ALU.subtract
                                  ).then_inc(S["cumc_done"], 1)

            def key_factors(n, first=False):
                dve.wait_ge(S["a_done"], n + 1)
                if not first:
                    dve.wait_ge(S["knew_done"], n)
                for i in range(HP):
                    dve.tensor_scalar(k_mix[:, i, :], a_t[:, i, :], hc[:, 0, i:i + 1], hc[:, 1, i:i + 1], ALU.mult, ALU.add
                                      ).then_inc(S["kmix_done"], 1)

            def gate_stats(n):
                dve.wait_ge(S["sg_tr"], n + 1)
                dve.bn_stats(bn[:, 0:6], ps[:, 7, :]).then_inc(S["sg_bn"], 1)
                dve.wait_ge(S["sg_bn"], n + 1)
                met(dve)
                dve.bn_aggr(bn[:, 6:8], bn[:, 0:6]).then_inc(S["sg_ag"], 1)

            def reciprocals(n, first=False):
                dve.wait_ge(S["kn_rt"], n + 1)
                dve.tensor_scalar(n8[0:RH, 0, :], n8[0:RH, 0, :], 1e-12, None, ALU.max).then_inc(S["kn_mx"], 1)
                dve.wait_ge(S["sg_rt"], n + 1)
                dve.reciprocal(bn[:, 9:10], bn[:, 8:9]).then_inc(S["sg_rc"], 1)
                dve.wait_ge(S["kn_mx"], n + 1)
                dve.reciprocal(n8[0:RH, 1, :], n8[0:RH, 0, :]).then_inc(S["kn_rc"], 1)
                dve.wait_ge(S["sg_rc"], n + 1)
                if not first:
                    dve.wait_ge(S["sg_lw"], n)
                dve.tensor_scalar(v_hat[:], ps[:, 7, :], bn[:, 6:7], bn[:, 9:10], ALU.subtract, ALU.mult).then_inc(S["sg_vh"], 1)

            def keys_normed(n, par):
                dve.wait_ge(S["kb_ps"], n + 1)
                dve.tensor_tensor(kk[:], zin[par][:, 4:8, :], bank4(6), ALU.mult).then_inc(S["kk_done"], 1)

            def decayed(n, par):
                dve.wait_ge(S["kk_done"], n + 1)
                dve.wait_ge(S["wexc_done"], n + 1)
                if used_before(n):
                    dve.wait_ge(S["y_ps"], n - 1)
                for e in range(2):
                    rows = slice(e * RN, (e + 1) * RN)
                    ins = dve.scalar_tensor_tensor(pairs_of(qr[par], 0, e), kk[rows], -1.0, w_exc[rows], ALU.mult, ALU.mult)
                    ins.then_inc(S["qq_done"] if e else S["qq0_done"], 1)
                dve.wait_ge(S["bv_done"], n + 1)
                dve.tensor_tensor(bt[:], b_vec[:], w_neg[:], ALU.mult).then_inc(S["bt_done"], 1)

            def bonuses(n, par, first=False):
                dve.wait_ge(S["bon_ps"], n + 1)
                if not first:
                    dve.wait_ge(S["bonus_done"], n)
                dve.tensor_tensor(bon_raw[:], zin[par][:, 8:12, :], bank4(7), ALU.mult).then_inc(S["bon_v"], 1)

            def mixed(n, first=False):
                dve.wait_ge(S["sg_ps"], n + 1)
                if not first:
                    dve.wait_ge(S["sg_out"], n)
                dve.tensor_tensor(s_mix[:], bsp[:], bank4(7), ALU.add).then_inc(S["sg_mx"], 1)

            def state_in(n, par, first=False):
                dve.wait_ge(S["wmid_done"], n + 1)
                if not first:
                    dve.wait_ge(S["h_new"], n)
                    dve.wait_ge(S["y_ps"], n)
                dve.tensor_tensor(h_0[:], h_st[:], w_mid[par][:].unsqueeze(2).to_broadcast([P, HP, RN]), ALU.mult
                                  ).then_inc(S["h0_done"], 1)

            def deviation(c):
                dve.wait_ge(S["yv_rt"], c + 1)
                dve.reciprocal(n8[0:RH, 4, :], n8[0:RH, 3, :]).then_inc(S["yv_rc"], 1)

            def normalised(c):
                dve.wait_ge(S["yb_ps"], c + 1)
                dve.tensor_tensor(y_n[:], y_cen[:], bank4(4), ALU.mult).then_inc(S["yn_done"], 1)

            def body(c, par, first=False, last=False):
                n, npar = c + 1, 1 - par
                take_scores(c, 0)
                take_scores(c, 1)
                if not last:
                    sum_decays(n)
                take_level(c, 1)
                if not last:
                    key_factors(n)
                take_level(c, 2)
                if not last:
                    gate_stats(n)
                take_level(c, 3)
                if not last:
                    reciprocals(n)
                take_level(c, 4)
                if not first:
                    deviation(c - 1)
                if not last:
                    keys_normed(n, npar)
                take_level(c, 5)
                if not last:
                    decayed(n, npar)
                if not first:
                    normalised(c - 1)
                take_level(c, 6)
                dve.wait_ge(S["rhs_ps"], c + 1)
                dve.tensor_copy(rhs_t[:].rearrange("p h r -> p (h r)"), ps[:, 4, :]).then_inc(S["rhs_ev"], 1)
                if not last:
                    bonuses(n, npar)
                    mixed(n)
                dve.wait_ge(S["h_ps"], c + 1)
                for e in range(2):
                    rows = slice(e * RN, (e + 1) * RN)
                    dve.tensor_tensor(h_1[rows], h_0[rows],
                                      ps[rows, 4, :].rearrange("p (m e r) -> p m e r", e=2, r=RN)[:, :, e, :], ALU.add
                                      ).then_inc(S["h_add"], 1)
                dve.wait_ge(S["h_add"], 2 * c + 2)
                dve.wait_ge(S["wend_done"], c + 1)
                dve.tensor_tensor(h_st[:], h_1[:], w_end[par][:].unsqueeze(2).to_broadcast([P, HP, RN]), ALU.mult
                                  ).then_inc(S["h_new"], 1)
                if not last:
                    state_in(n, npar)

            sum_decays(0, True)
            key_factors(0, True)
            gate_stats(0)
            reciprocals(0, True)
            keys_normed(0, 0)
            dve.wait_ge(S["rconst_done"], N_SET)
            decayed(0, 0)
            bonuses(0, 0, True)
            mixed(0, True)
            state_in(0, 0, True)
            body(0, 0, first=True)
            with dve.Fori(0, CHUNKS // 2 - 1) as i:
                body(2 * i + 1, 1)
                body(2 * i + 2, 0)
            body(CHUNKS - 1, 1, last=True)
            deviation(CHUNKS - 1)
            dve.wait_ge(S["yb_done"], CHUNKS - 1)
            normalised(CHUNKS - 1)

            dve.wait_ge(S["yo_done"], CHUNKS)
            dve.wait_ge(S["yn_done"], CHUNKS)

            dve.sem_inc(S["mixers_done"], 1)

            def y_lo(hf):
                for k in range(KT):
                    dve.wait_ge(S["act_hi"], KT * (1 + HALVES) + 3 * KT * hf + k + 1)
                    dve.tensor_tensor(a_lo[:, k, :], y_in_raw[:, k, :], a_hi[:, k, :].bitcast(F32), ALU.subtract
                                      ).then_inc(S["act_lo"], 1)

            y_lo(0)
            for hf in range(HALVES):
                q0 = Q_TAIL + hf * PAIRS_TAIL
                n0 = 1 + HALVES + 3 * hf
                hi0 = KT * (1 + HALVES) + 3 * KT * hf
                def at_k(t, k):
                    return t[:, k:k + 1, :] if isinstance(k, int) else t[:, ds(k, 1), :]

                def add_x(pair, u, k, done):
                    dve.wait_ge(S["job_done"], 2 * pair + u + 1)
                    dve.tensor_tensor(at_k(x, k), flat(slot(u)).unsqueeze(1), at_k(x, k), ALU.add).then_inc(S["job_out"], 1)
                    if done:
                        dve.wait_ge(S["job_out"], 2 * pair + u + 1)
                        dve.sem_inc(S["x_new"], 1)

                def residual(n, first_q, hi_t, lo_t, g):
                    with dve.Fori(0, PAIRS_OUT) as i:
                        for u in range(2):
                            k = 2 * i + u
                            if n == 0:
                                dve.wait_ge(S[f"xr_in{u}"], 16 * (hf * (KT // 2) + i + 1))
                                met(dve)
                            add_x(first_q + i, u, k, True)
                            dve.wait_ge(S["act_hi"], hi0 + (n + 1) * KT + k + 1)
                            dve.scalar_tensor_tensor(at_k(lo_t, k), at_k(x, k), gain[:, g, ds(k, 1)], at_k(hi_t, k).bitcast(F32),
                                                     ALU.mult, ALU.subtract).then_inc(S["act_lo"], 1)

                residual(0, q0, b_hi, b_lo, G_ATT)
                root_to_rstd(n0)
                with dve.Fori(0, PAIRS_OUT) as i:
                    for u in range(2):
                        dve.wait_ge(S["job_done"], 2 * (q0 + PAIRS_OUT + i) + u + 1)
                        dve.tensor_tensor(q[:, ds(2 * i + u, 1), :], flat(slot(u)).unsqueeze(1), rstd[:].unsqueeze(1), ALU.mult
                                          ).then_inc(S["job_out"], 1)

                def maxima(unit):
                    b0, c0 = 2 * (unit % 2), 4 * (unit % 2)
                    dve.wait_ge(S["s_ps"], hf * 8 + unit + 1)
                    dve.tensor_reduce(stat_m[:, c0:c0 + 4], ps[:, b0:b0 + 2, :].rearrange("p a (t m) -> p (a t) m", m=MEM),
                                      mybir.AxisListType.X, ALU.max).then_inc(S["s_max"], 1)
                    dve.wait_ge(S["s_max"], hf * 8 + unit + 1)
                    if unit >= 2:
                        dve.wait_ge(S["s_exp"], 4 * (hf * 8 + unit - 1))
                    dve.tensor_scalar(stat_n[:, c0:c0 + 4], stat_m[:, c0:c0 + 4], -float(XD) ** -0.5, None, ALU.mult
                                      ).then_inc(S["s_neg"], 1)

                def normalise(unit):
                    c0 = 4 * (unit % 2)
                    dve.wait_ge(S["s_exp"], 4 * (hf * 8 + unit + 1))
                    dve.reciprocal(stat_r[:, c0:c0 + 4], stat_s[:, c0:c0 + 4]).then_inc(S["s_rcp"], 1)
                    dve.wait_ge(S["s_rcp"], hf * 8 + unit + 1)
                    for t in range(4):
                        dve.tensor_scalar(prob[:, unit % 2, t, :], prob[:, unit % 2, t, :], stat_r[:, c0 + t:c0 + t + 1], None,
                                          ALU.mult).then_inc(S["s_nrm"], 1)

                def out_lo(unit):
                    h, nb = unit // NB, unit % NB
                    cols = slice(nb * BANK, (nb + 1) * BANK)
                    dve.wait_ge(S["o_hi"], hf * 8 + unit + 1)
                    dve.tensor_tensor(b_lo[:, 2 * h:2 * h + 2, cols], ps[:, 6:8, :], b_hi[:, 2 * h:2 * h + 2, cols].bitcast(F32),
                                      ALU.subtract).then_inc(S["o_lo"], 1)

                maxima(0)
                maxima(1)
                normalise(0)
                for unit in range(8):
                    if unit < 7:
                        normalise(unit + 1)
                    if unit < 6:
                        maxima(unit + 2)
                    out_lo(unit)
                residual(1, q0 + 2 * PAIRS_OUT, a_hi, a_lo, G_FF)
                root_to_rstd(n0 + 1)

                def gated(pair, f_all, f):
                    done = hf * FF_TILES + f_all
                    dve.wait_ge(S["job_done"], 2 * pair + 1)
                    dve.tensor_tensor(work[:, 0, :], flat(slot(0)), rstd[:], ALU.mult).then_inc(S["job_out"], 1)
                    dve.wait_ge(S["job_out"], 2 * pair + 1)
                    dve.sem_inc(S["gate_s"], 1)
                    dve.wait_ge(S["job_done"], 2 * pair + 2)
                    dve.tensor_tensor(sq[:], flat(slot(1)), rstd[:], ALU.mult).then_inc(S["job_out"], 1)
                    dve.wait_ge(S["job_out"], 2 * pair + 2)
                    dve.wait_ge(S["gate_a"], done + 1)
                    dve.tensor_tensor(work[:, 1, :], work[:, 0, :], sq[:], ALU.mult).then_inc(S["prod"], 1)
                    dve.wait_ge(S["prod_hi"], done + 1)
                    dve.tensor_tensor(at_k(b_lo, f), work[:, 1:2, :], at_k(b_hi, f).bitcast(F32), ALU.subtract).then_inc(S["prod_lo"], 1)
                    dve.wait_ge(S["prod_lo"], done + 1)

                at_q, f0 = 3 * PAIRS_OUT, 0
                for gi, n in enumerate(FF_GROUPS):
                    with dve.Fori(0, n) as i:
                        gated(q0 + at_q + i, f0 + i, i)
                    last = gi == len(FF_GROUPS) - 1
                    with dve.Fori(0, PAIRS_OUT - last) as i:
                        for u in range(2):
                            add_x(q0 + at_q + n + i, u, 2 * i + u, last)
                            if not last:
                                dve.wait_ge(S["job_out"], 2 * (q0 + at_q + n + i) + u + 1)
                    if last:
                        if hf == 0:
                            y_lo(1)
                        for u in range(2):
                            add_x(q0 + PAIRS_TAIL - 1, u, KT - 2 + u, True)
                    at_q += n + PAIRS_OUT
                    f0 += n
                root_to_rstd(n0 + 2)
                with dve.Fori(0, KT // 2) as i:
                    for u in range(2):
                        k = 2 * i + u
                        dve.wait_ge(S[f"fin_st{u}"], 16 * (1 + hf * (KT // 2) + i))
                        dve.scalar_tensor_tensor(work[:, u:u + 1, :], x[:, ds(k, 1), :], gain[:, G_FINAL, ds(k, 1)],
                                                 rstd[:].unsqueeze(1), ALU.mult, ALU.mult).then_inc(S["fin"], 1)


def kernel(x, mem, norm1_g, w_in, shift_mu, w0, w_lora_up, a0, a_lora_up, g_lora_up, k_k, k_a, r_k, lnx_w, lnx_b,
           sgu_ln_w, sgu_ln_b, w_spatial, b_spatial, w_out, norm2_g, mem_norm_g, wq_x, wk_x, wv_x, wo_x, norm3_g,
           w_gate, w_up, w_down, norm_f_g):
    import numpy as np
    import concourse.bacc as bacc
    from concourse.bass_utils import run_bass_kernel_spmd as run

    A = np.ascontiguousarray
    arrays = {}
    arrays["xT"] = A(np.asarray(x)[0].T).reshape(KT, P, T)
    arrays["memT"] = A(np.asarray(mem)[0].T).reshape(KT, P, MEM)
    col = lambda g: np.asarray(g).reshape(-1, P).T
    arrays["gains"] = A(np.stack([col(norm1_g[0]), col(norm2_g[0]), col(norm3_g[0]), col(norm_f_g), col(mem_norm_g[0])], 1))

    def tiles(w):
        w = np.asarray(w)
        return w.reshape(w.shape[0] // P, P, w.shape[1] // P, P).transpose(2, 1, 0, 3)

    gate_t, up_t, down_t = tiles(w_gate[0]), tiles(w_up[0]), tiles(w_down[0])
    rows = [tiles(wk_x[0]), tiles(wv_x[0]), tiles(w_in[0]), tiles(w_out[0]), tiles(wq_x[0]), tiles(wo_x[0])]
    f0 = 0
    for n in FF_GROUPS:
        pair = np.stack([gate_t[f0:f0 + n], up_t[f0:f0 + n]], 1)
        rows.append(pair.reshape(2 * n, P, KT, P))
        down = np.zeros((D // P, P, KT, P), np.float32)
        down[:, :, 0:n] = down_t[:, :, f0:f0 + n]
        rows.append(down)
        f0 += n
    weights = np.concatenate(rows, 0)
    arrays["weights"] = A(weights.reshape(weights.shape[0], P, KT * P))
    arrays["shift_mu"] = A(col(shift_mu[0]))

    def padded(*parts):
        parts = np.concatenate([np.asarray(r) for r in parts], 0)
        out = np.zeros((P,) + parts.shape[1:], np.float32)
        out[:parts.shape[0]] = parts
        return out

    arrays["w_lora"] = padded(w_lora_up[0], w0[0][None])
    arrays["a_lora"] = padded(a_lora_up[0], a0[0][None])
    arrays["g_lora"] = A(np.asarray(g_lora_up[0]))
    arrays["head_cols"] = A(np.stack([col(k_a[0]), np.zeros((P, HP), np.float32), col(lnx_b[0])], 1))

    def on_rows(g):
        out = np.zeros((RH, HP, 2, RN), np.float32)
        for h in range(RH):
            out[h, h // 2, h % 2] = np.asarray(g).reshape(RH, RN)[h]
        return out.reshape(RH, HP, P)

    def on_cols(g):
        return A(on_rows(g).transpose(2, 1, 0))

    arrays["kk_rows"], arrays["lnx_rows"] = padded(on_rows(k_k[0])), padded(on_rows(lnx_w[0]))
    arrays["kk_cols"] = on_cols(k_k[0])
    spread = np.zeros((2, RN, HP, 2, RN), np.float32)
    for e in range(2):
        spread[e, :, :, e, :] = np.asarray(r_k[0]).reshape(HP, 2, RN)[:, e].T[:, :, None]
    arrays["rk_spread"] = spread.reshape(P, HP, P)
    arrays["w_spatialT"] = A(np.asarray(w_spatial[0]).transpose(2, 0, 1))
    arrays["b_spatial"] = A(np.asarray(b_spatial[0]).reshape(HP, 2, L).transpose(1, 0, 2))
    arrays["sgu_ln"] = A(np.stack([np.asarray(sgu_ln_w[0]), np.asarray(sgu_ln_b[0])]))
    f32 = np.float32
    arrays["consts"] = A(np.stack([np.eye(P, dtype=f32), np.ones((P, P), f32)], 1))
    arrays["cen"] = np.kron(np.eye(2), np.eye(RN) - 1.0 / RN).astype(f32)
    arrays["head_mean"] = on_cols(np.full((RH, RN), 1.0 / RN, f32))
    reset = np.ones((P, HP, L), f32)
    reset[:, :, 0] = 0
    arrays["scan_reset"] = reset.reshape(P, HP * L)
    i = np.arange(L)
    low = np.zeros((P, len(LEVELS), RN), f32)
    for n, b in enumerate(LEVELS):
        same = (i[:, None] // (2 * b)) == (i[None, :] // (2 * b))
        is_left = (i // b) % 2 == 0
        low[:, n] = (same & is_left[:, None])[:, ~is_left]
    arrays["block_masks"] = low
    arrays["tri_masks"] = np.stack([i[:, None] < i[None, :], i[:, None] <= i[None, :]], 1).astype(f32)

    nc = bacc.Bacc("TRN2", target_bir_lowering=False, num_devices=1)
    ins = {}
    for name, a in arrays.items():
        dt = mybir.dt.from_np(a.dtype)
        ins[name] = nc.dram_tensor(f"in_{name}", a.shape, dt, kind="ExternalInput").ap()
    out = nc.dram_tensor("outT", (KT, P, T), F32, kind="ExternalOutput").ap()
    hybrid_block_kernel(nc, outT=out, **ins)
    r = run(nc, [{f"in_{k}": v for k, v in arrays.items()}], core_ids=[0])
    return A(r.results[0]["outT"].reshape(D, T).T)[None]
```
